# Optimizing a Trainium2 kernel written in Bass

```python
import jax
import jax.numpy as jnp
from jax import lax
import numpy as np

D_MODEL = 2048
BATCH = 1
SEQ = 256
DEPTH = 2

N_HEADS = 32
HEAD_DIM = 64
SWA_KV_HEADS = 4
SWA_WINDOW = 128
Q_BLOCK = 128
NSA_KV_HEADS = 4
CMP_LEN = 32
CMP_STRIDE = 16
CMP_HIDDEN = 512
SEL_LEN = 64
SEL_TOPK = 16
NSA_WINDOW = 512
D_FF = 5632
CONV_WIDTH = 3
RMS_EPS = 1e-6
MASK_VALUE = -1e30
FORCE_VALUE = 1e30
N_MIXERS = 2
N_SWA_LAYERS = (DEPTH + 1) // 2
N_NSA_LAYERS = DEPTH // 2
SWA_IN = N_HEADS * HEAD_DIM + 2 * SWA_KV_HEADS * HEAD_DIM
NSA_IN = N_HEADS * HEAD_DIM + 6 * NSA_KV_HEADS * HEAD_DIM + 3 * N_HEADS
F32 = jnp.float32

kernel_name = 'hybrid_swa_sink_nsa_convffn'

def rmsnorm(x, g):
    xf = x.astype(F32)
    y = xf * lax.rsqrt(jnp.mean(xf * xf, axis=-1, keepdims=True) + RMS_EPS)
    return (y * g.astype(F32)).astype(x.dtype)

def alibi_slopes(n):
    return jnp.exp2(-8.0 * jnp.arange(1, n + 1, dtype=F32) / n)

def masked_softmax(s, valid):
    s = jnp.where(valid, s, MASK_VALUE)
    m = jnp.max(s, axis=-1, keepdims=True)
    e = jnp.where(valid, jnp.exp(s - m), 0.0)
    return e / jnp.maximum(jnp.sum(e, axis=-1, keepdims=True), 1e-30)

def swa_sink_attention(h, w_in, b_in, sinks, w_o, b_o):
    B, S, _ = h.shape
    G = N_HEADS // SWA_KV_HEADS
    nb = S // Q_BLOCK
    proj = h @ w_in + b_in
    q, k, v = jnp.split(proj, [N_HEADS * HEAD_DIM, (N_HEADS + SWA_KV_HEADS) * HEAD_DIM], axis=-1)
    q = q.reshape(B, nb, Q_BLOCK, SWA_KV_HEADS, G, HEAD_DIM).astype(F32) * HEAD_DIM ** -0.5
    k = k.reshape(B, nb, Q_BLOCK, SWA_KV_HEADS, HEAD_DIM).astype(F32)
    v = v.reshape(B, nb, Q_BLOCK, SWA_KV_HEADS, HEAD_DIM).astype(F32)

    def with_prev(t):
        prev = jnp.pad(t[:, :-1], ((0, 0), (1, 0), (0, 0), (0, 0), (0, 0)))
        return jnp.concatenate([prev, t], axis=2)

    kk, vv = with_prev(k), with_prev(v)
    s = jnp.einsum('bnqkgd,bnskd->bnkgqs', q, kk)
    dist = Q_BLOCK + jnp.arange(Q_BLOCK)[:, None] - jnp.arange(2 * Q_BLOCK)[None, :]
    band = (dist >= 0) & (dist < SWA_WINDOW)
    key_pos = jnp.arange(nb)[:, None] * Q_BLOCK - Q_BLOCK + jnp.arange(2 * Q_BLOCK)[None, :]
    valid = band[None] & (key_pos >= 0)[:, None, :]
    slopes = alibi_slopes(N_HEADS).reshape(SWA_KV_HEADS, G)
    s = s - slopes[:, :, None, None] * dist.astype(F32)
    s = jnp.where(valid[:, None, None], s, MASK_VALUE)
    sink = sinks.astype(F32).reshape(SWA_KV_HEADS, G)[:, :, None]
    m = jnp.maximum(jnp.max(s, axis=-1), sink)
    e = jnp.exp(s - m[..., None])
    p = e / (jnp.sum(e, axis=-1, keepdims=True) + jnp.exp(sink - m)[..., None])
    o = jnp.einsum('bnkgqs,bnskd->bnqkgd', p, vv).reshape(B, S, N_HEADS * HEAD_DIM).astype(h.dtype)
    return o @ w_o + b_o

def compress_blocks(kv, pe, w1, b1, w2, b2):
    B, S, G, Dh = kv.shape
    n_cmp = (S - CMP_LEN) // CMP_STRIDE + 1
    idx = jnp.arange(n_cmp)[:, None] * CMP_STRIDE + jnp.arange(CMP_LEN)[None, :]
    blk = kv[:, idx] + pe[None, None, :, None, :]
    blk = blk.transpose(0, 1, 3, 2, 4).reshape(B, n_cmp, G, CMP_LEN * Dh)
    return jax.nn.gelu(blk @ w1 + b1) @ w2 + b2

def cmp_sel_overlap(S):
    n_cmp = (S - CMP_LEN) // CMP_STRIDE + 1
    cs = np.arange(n_cmp) * CMP_STRIDE
    ss = np.arange(S // SEL_LEN) * SEL_LEN
    ov = (cs[:, None] < ss[None, :] + SEL_LEN) & (cs[:, None] + CMP_LEN > ss[None, :])
    return jnp.asarray(ov.astype(np.float32))

def nsa_attention(h, w_in, cmp_pe, cmp_w1, cmp_b1, cmp_w2, cmp_b2, w_o):
    B, S, _ = h.shape
    G = NSA_KV_HEADS
    R = N_HEADS // G
    HD = N_HEADS * HEAD_DIM
    KD = G * HEAD_DIM
    proj = h @ w_in
    splits = [HD + i * KD for i in range(7)]
    q, kc, vc, ks, vs, kw, vw, gate = jnp.split(proj, splits, axis=-1)
    q = q.reshape(B, S, G, R, HEAD_DIM).astype(F32) * HEAD_DIM ** -0.5

    def to_kv(t):
        return t.reshape(B, S, G, HEAD_DIM)

    k_cmp = compress_blocks(to_kv(kc), cmp_pe[0], cmp_w1[0], cmp_b1[0], cmp_w2[0], cmp_b2[0]).astype(F32)
    v_cmp = compress_blocks(to_kv(vc), cmp_pe[1], cmp_w1[1], cmp_b1[1], cmp_w2[1], cmp_b2[1]).astype(F32)
    n_cmp = k_cmp.shape[1]
    cmp_end = jnp.arange(n_cmp) * CMP_STRIDE + CMP_LEN - 1
    overlap = cmp_sel_overlap(S)
    n_sel = S // SEL_LEN
    topk = min(SEL_TOPK, n_sel)
    k_sel = to_kv(ks).astype(F32).reshape(B, n_sel, SEL_LEN, G, HEAD_DIM).transpose(0, 3, 1, 2, 4)
    v_sel = to_kv(vs).astype(F32).reshape(B, n_sel, SEL_LEN, G, HEAD_DIM).transpose(0, 3, 1, 2, 4)
    pad = ((0, 0), (NSA_WINDOW, 0), (0, 0), (0, 0))
    k_win = jnp.pad(to_kv(kw).astype(F32), pad)
    v_win = jnp.pad(to_kv(vw).astype(F32), pad)
    gates = jax.nn.sigmoid(gate.astype(F32)).reshape(B, S, G, R, 3)
    slopes = alibi_slopes(N_HEADS).reshape(G, R)
    bi = jnp.arange(B)[:, None, None, None]
    gi = jnp.arange(G)[None, :, None, None]
    sel_ids = jnp.arange(n_sel)
    sel_off = jnp.arange(SEL_LEN)
    win_off = jnp.arange(Q_BLOCK + NSA_WINDOW)
    q_idx = jnp.arange(Q_BLOCK)

    def query_block(c):
        t0 = c * Q_BLOCK
        t = t0 + q_idx
        qc = lax.dynamic_slice_in_dim(q, t0, Q_BLOCK, axis=1)
        gc = lax.dynamic_slice_in_dim(gates, t0, Q_BLOCK, axis=1)
        d_cmp = t[:, None] - cmp_end[None, :]
        s = jnp.einsum('bqgrd,bngd->bgrqn', qc, k_cmp) - slopes[:, :, None, None] * d_cmp.astype(F32)
        p_cmp = masked_softmax(s, d_cmp >= 0)
        o_cmp = jnp.einsum('bgrqn,bngd->bqgrd', p_cmp, v_cmp)
        imp = jnp.einsum('bgrqn,nj->bgqj', p_cmp, overlap)
        cur = t // SEL_LEN
        causal = sel_ids[None, :] <= cur[:, None]
        forced = (sel_ids[None, :] == 0) | (sel_ids[None, :] == cur[:, None]) | (sel_ids[None, :] == cur[:, None] - 1)
        score = jnp.where(forced, FORCE_VALUE, jnp.where(causal, imp, MASK_VALUE))
        _, top = lax.top_k(score, topk)
        kg = k_sel[bi, gi, top].reshape(B, G, Q_BLOCK, topk * SEL_LEN, HEAD_DIM)
        vg = v_sel[bi, gi, top].reshape(B, G, Q_BLOCK, topk * SEL_LEN, HEAD_DIM)
        pos = (top[..., None] * SEL_LEN + sel_off).reshape(B, G, Q_BLOCK, topk * SEL_LEN)
        blk_ok = jnp.repeat(top <= cur[None, None, :, None], SEL_LEN, axis=-1)
        d_sel = t[None, None, :, None] - pos
        valid_sel = (d_sel >= 0) & blk_ok
        s = jnp.einsum('bqgrd,bgqsd->bgrqs', qc, kg) - slopes[None, :, :, None, None] * d_sel[:, :, None].astype(F32)
        p = masked_softmax(s, valid_sel[:, :, None])
        o_sel = jnp.einsum('bgrqs,bgqsd->bqgrd', p, vg)
        kwc = lax.dynamic_slice_in_dim(k_win, t0, Q_BLOCK + NSA_WINDOW, axis=1)
        vwc = lax.dynamic_slice_in_dim(v_win, t0, Q_BLOCK + NSA_WINDOW, axis=1)
        d_win = q_idx[:, None] + NSA_WINDOW - win_off[None, :]
        key_pos = t0 - NSA_WINDOW + win_off
        valid_win = (d_win >= 0) & (d_win < NSA_WINDOW) & (key_pos >= 0)[None, :]
        s = jnp.einsum('bqgrd,bsgd->bgrqs', qc, kwc) - slopes[:, :, None, None] * d_win.astype(F32)
        p = masked_softmax(s, valid_win)
        o_win = jnp.einsum('bgrqs,bsgd->bqgrd', p, vwc)
        o = gc[..., 0:1] * o_cmp + gc[..., 1:2] * o_sel + gc[..., 2:3] * o_win
        return o.reshape(B, Q_BLOCK, HD)

    out = lax.map(query_block, jnp.arange(S // Q_BLOCK))
    out = out.transpose(1, 0, 2, 3).reshape(B, S, HD).astype(h.dtype)
    return out @ w_o

def causal_dwconv(a, w, b):
    S = a.shape[1]
    ap = jnp.pad(a, ((0, 0), (CONV_WIDTH - 1, 0), (0, 0)))
    y = b + ap[:, 0:S] * w[0]
    for kk in range(1, CONV_WIDTH):
        y = y + ap[:, kk:kk + S] * w[kk]
    return y

def conv_ffn(h, w_gate, w_up, conv_w, conv_b, w_down):
    a = causal_dwconv(h @ w_gate, conv_w, conv_b)
    return (jax.nn.silu(a) * (h @ w_up)) @ w_down

def setup_inputs(seed: int = 0) -> dict:
    key = jax.random.key(seed)
    ks = iter(jax.random.split(key, 32))

    def rnd(shape, scale):
        return jax.random.normal(next(ks), shape, jnp.float32) * scale

    HD = N_HEADS * HEAD_DIM
    return {
        'x': rnd((BATCH, SEQ, D_MODEL), 1.0),
        'norm_g': 1.0 + rnd((DEPTH, 4, D_MODEL), 0.02),
        'swa_w_in': rnd((N_SWA_LAYERS, D_MODEL, SWA_IN), D_MODEL ** -0.5),
        'swa_b_in': rnd((N_SWA_LAYERS, SWA_IN), 0.02),
        'swa_sinks': rnd((N_SWA_LAYERS, N_HEADS), 0.5),
        'swa_w_o': rnd((N_SWA_LAYERS, HD, D_MODEL), HD ** -0.5),
        'swa_b_o': rnd((N_SWA_LAYERS, D_MODEL), 0.02),
        'nsa_w_in': rnd((N_NSA_LAYERS, D_MODEL, NSA_IN), D_MODEL ** -0.5),
        'nsa_cmp_pe': rnd((N_NSA_LAYERS, 2, CMP_LEN, HEAD_DIM), 0.1),
        'nsa_cmp_w1': rnd((N_NSA_LAYERS, 2, CMP_LEN * HEAD_DIM, CMP_HIDDEN), (CMP_LEN * HEAD_DIM) ** -0.5),
        'nsa_cmp_b1': rnd((N_NSA_LAYERS, 2, CMP_HIDDEN), 0.02),
        'nsa_cmp_w2': rnd((N_NSA_LAYERS, 2, CMP_HIDDEN, HEAD_DIM), CMP_HIDDEN ** -0.5),
        'nsa_cmp_b2': rnd((N_NSA_LAYERS, 2, HEAD_DIM), 0.02),
        'nsa_w_o': rnd((N_NSA_LAYERS, HD, D_MODEL), HD ** -0.5),
        'ffn_w_gate': rnd((DEPTH, D_MODEL, D_FF), D_MODEL ** -0.5),
        'ffn_w_up': rnd((DEPTH, D_MODEL, D_FF), D_MODEL ** -0.5),
        'ffn_conv_w': rnd((DEPTH, CONV_WIDTH, D_FF), CONV_WIDTH ** -0.5),
        'ffn_conv_b': rnd((DEPTH, D_FF), 0.02),
        'ffn_w_down': rnd((DEPTH, D_FF, D_MODEL), D_FF ** -0.5),
    }

def reference(x, norm_g, swa_w_in, swa_b_in, swa_sinks, swa_w_o, swa_b_o,
              nsa_w_in, nsa_cmp_pe, nsa_cmp_w1, nsa_cmp_b1, nsa_cmp_w2, nsa_cmp_b2, nsa_w_o,
              ffn_w_gate, ffn_w_up, ffn_conv_w, ffn_conv_b, ffn_w_down):
    for i in range(DEPTH):
        g = norm_g[i]
        h = rmsnorm(x, g[0])
        j = i // N_MIXERS
        if i % N_MIXERS == 0:
            mix = swa_sink_attention(h, swa_w_in[j], swa_b_in[j], swa_sinks[j], swa_w_o[j], swa_b_o[j])
        else:
            mix = nsa_attention(h, nsa_w_in[j], nsa_cmp_pe[j], nsa_cmp_w1[j], nsa_cmp_b1[j],
                                nsa_cmp_w2[j], nsa_cmp_b2[j], nsa_w_o[j])
        x = x + rmsnorm(mix, g[1])
        h = rmsnorm(x, g[2])
        x = x + rmsnorm(conv_ffn(h, ffn_w_gate[i], ffn_w_up[i], ffn_conv_w[i], ffn_conv_b[i], ffn_w_down[i]), g[3])
    return x


_drawn_inputs = setup_inputs


def setup_inputs(seed=0):
    import zlib

    import numpy as np

    out = dict(_drawn_inputs(seed))
    spreads = {}
    factors = {'nsa_cmp_b1': 6.862, 'nsa_cmp_b2': 4.131, 'ffn_conv_b': 3.557}
    for name, (base, spread) in spreads.items():
        noise = np.random.default_rng([zlib.crc32(name.encode()), seed]).standard_normal(out[name].shape)
        drawn = base * np.exp(spread * noise) if base else spread * noise
        out[name] = jnp.asarray(drawn.astype(out[name].dtype))
    for name, factor in factors.items():
        out[name] = (out[name] * factor).astype(out[name].dtype)
    return out
```

```python
from contextlib import ExitStack

import numpy as np

import concourse.bass as bass
from concourse import mybir

F32 = mybir.dt.float32
F32R = mybir.dt.float32r
ALU = mybir.AluOpType
ACT = mybir.ActivationFunctionType

P = 128
S = 256
D = 2048
F = 5632
HD = 64
NH = 32
GROUPS = 4
HPG = NH // GROUPS
KT = D // P
FT = F // P
UNIT = 512
UT = UNIT // P
NF = F // UNIT
CK = 2
CW = CK * UNIT
RING = 4
CH = KT // CK
CHF = FT // CK
WINDOW = 128
CMP_LEN, CMP_STRIDE = 32, 16
NC = (S - CMP_LEN) // CMP_STRIDE + 1
EPS = 1e-6
FAR = 1e30
NO_KEY = 1e20
CAUSAL = S // 2 * 3
TT = S // P

KV0, Q0, O0, FF0, DN0 = 0, 1, 5, 9, 31
KC1, KS1, KW1, WK1, WV1, Q1, O1, FF1, DN1 = 35, 36, 37, 38, 39, 40, 44, 48, 70
UNITS = 74

LAG = 3


def first_chunk(u):
    longer = min(max(u - DN0, 0), 4) + min(max(u - DN1, 0), 4)
    return CH * u + (CHF - CH) * longer


CHUNKS = first_chunk(UNITS)


def attention_items(layer):
    if layer == 0:
        return [(i, "swa") for i in range(HPG)]
    return [(i, k) for i in range(HPG) for k in ("sel", "win", "cmp")]


def attention_slots(layer, last):
    steps = len(attention_items(layer)) + LAG + 2
    lo, hi = (0, 23) if last else (1, 30)
    at = [[] for _ in range(CH * UT)]
    for s in range(steps):
        at[lo + s * (hi - lo) // (steps - 1)].append(s)
    return at


def build_program(nc, x, gains, stream, b_in, b_o, sinks, conv, pe, b1, w2, b2k, b2v, w_gates, out):
    with ExitStack() as ctx:
        def sb(name, shape, dt=F32, c=ctx):
            return c.enter_context(nc.sbuf_tensor(name, [P] + shape if isinstance(shape, list) else shape, dt))

        def sem(name):
            return ctx.enter_context(nc.semaphore(name))

        sets = [ctx.enter_context(nc.psum_tensor(f"set{i}", [P, UT, 512], F32)) for i in range(2)]
        ps_scores = [sets[1][:, 0, :], sets[1][:, 1, :]]
        ps_turned = sets[1][:, 2, :]
        ps_o = sets[1][:, 3, :]
        ps_mean = [sets[0][:, 0, 0:S], sets[0][:, 1, 0:S]]

        raw = sb("raw", [RING, CW])
        whi = sb("whi", [RING, CW], F32R)
        wlo = sb("wlo", [RING, CW], F32R)
        xT = sb("xT", [KT, S])
        half = sb("half", [2, UT, S])
        ones = sb("ones", [P])
        ident = sb("ident", [P])
        root = sb("root", [S])
        rnorm = sb("rnorm", [S])
        g_sb = sb("g_sb", [8, KT])
        conv_sb = sb("conv_sb", [2, NF, 4 * UT])
        b_in_sb = sb("b_in_sb", [20])
        b_q = sb("b_q", [16])
        b_o_sb = sb("b_o_sb", [KT])
        sinks_sb = sb("sinks_sb", [NH])
        neg_sinks = sb("neg_sinks", [NH])
        b1_sb = sb("b1_sb", [2, UT])
        b2k_sb = sb("b2k_sb", [1])
        b2v_sb = sb("b2v_sb", [HD])
        pe_sb = sb("pe_sb", [2, CMP_LEN])
        eps = sb("eps", [1])

        with ExitStack() as c:
            hs = sb("hs", [KT, 2 * S], F32R, c)
        with ExitStack() as c:
            y = sb("y", [KT, S], F32, c)
            squares = sb("squares", [2, UT, S], F32, c)
            sq_sum = sb("sq_sum", [UT, S], F32, c)
            pad = sb("pad", [UT, S], F32, c)
            del pad
        hold = ctx.enter_context(nc.sbuf_tensor("hold_h", [P, KT * 2 * S], F32R))
        del hold

        with ExitStack() as c:
            hid = sb("hid", [FT, 2 * S], F32R, c)
            gate_in = sb("gate_in", [UT, S + 2], F32, c)
            gate = sb("gate", [UT, S], F32, c)
            cw = sb("cw", [UT, 4], F32, c)
        with ExitStack() as c:
            with ExitStack() as c2:
                os_ = sb("os", [KT, 2 * S], F32R, c2)
            with ExitStack() as c2:
                wg_split = sb("wg_split", [KT, 2, 96], F32R, c2)
                blocks = [sb(f"blocks{i}", [KT, 2, GROUPS * NC], F32R, c2) for i in range(2)]
                kc_raw = sb("kc_raw", [2, 2, S], F32, c2)
            sb("hold_o", [KT * 2 * S], F32R, c)
            with ExitStack() as c2:
                qg = sb("qg", [UT, S], F32, c2)
            with ExitStack() as c2:
                block_f = sb("block_f", [KT, GROUPS * NC], F32, c2)
            sb("hold_q", [UT * S], F32, c)
            k_raw = sb("k_raw", [2, 2, S], F32, c)
            v_raw = sb("v_raw", [2, 2, S], F32, c)
            k_dup = sb("k_dup", [2, GROUPS, S], F32, c)
            v_nat = sb("v_nat", [2, TT, S], F32, c)
            k_g = sb("k_g", [2, S], F32, c)
            v_g = sb("v_g", [2, TT, HD], F32, c)
            kc_all = sb("kc_all", [GROUPS * NC], F32, c)
            vc_all = sb("vc_all", [GROUPS * HD], F32, c)
            kc_g = sb("kc_g", [NC], F32, c)
            vc_g = sb("vc_g", [HD], F32, c)
            gates = sb("gates", [TT, 96], F32, c)
            gates_g = sb("gates_g", [TT, 24], F32, c)
            sinks_g = sb("sinks_g", [HPG], F32, c)
            neg_sinks_g = sb("neg_sinks_g", [HPG], F32, c)
            dist = sb("dist", [CAUSAL], F32, c)
            bias = sb("bias", [HPG, CAUSAL], F32, c)
            bias_c = sb("bias_c", [HPG, 2 * NC], F32, c)
            with ExitStack() as c2:
                scored = sb("scored", [2, CAUSAL], F32, c2)
                probs = sb("probs", [LAG, CAUSAL], F32, c2)
                turned = sb("turned", [2, CAUSAL], F32, c2)
            with ExitStack() as c2:
                wg_raw = sb("wg_raw", [KT, 96], F32, c2)
            sb("hold_s", [(4 + LAG) * CAUSAL], F32, c)
            neg_max = sb("neg_max", [2, TT], F32, c)
            sums = sb("sums", [2, TT], F32, c)
            sink_e = sb("sink_e", [2, TT], F32, c)
            total = sb("total", [2, TT], F32, c)
            recip = sb("recip", [2, TT], F32, c)
            cmp_z = sb("cmp_z", [UT, GROUPS * NC], F32, c)
            cmp_h = sb("cmp_h", [2, UT, GROUPS * NC], F32, c)
            w2k_sb = sb("w2k_sb", [UT, P], F32, c)
            w2v_sb = sb("w2v_sb", [UT, HD], F32, c)

        raw_in = [sem(f"raw_in{i}") for i in range(RING)]
        hi_ready, lo_ready, chunk_used = sem("hi_ready"), sem("lo_ready"), sem("chunk_used")
        half_ready, evacuated = sem("half_ready"), sem("evacuated")
        const_in, late_in, x_in, filled = sem("const_in"), sem("late_in"), sem("x_in"), sem("filled")
        prepared = sem("prepared")
        x_ready, sq_ready, sq_used, mean_ready = sem("x_ready"), sem("sq_ready"), sem("sq_used"), sem("mean_ready")
        root_ready, rnorm_ready = sem("root_ready"), sem("rnorm_ready")
        hf_ready, h_hi_ready, h_ready = sem("hf_ready"), sem("h_hi_ready"), sem("h_ready")
        y_sq_ready, sq_sum_ready, y_scaled = sem("y_sq_ready"), sem("sq_sum_ready"), sem("y_scaled")
        k_dup_ready, v_turned, v_ready = sem("k_dup_ready"), sem("v_turned"), sem("v_ready")
        staged, bias_ready = sem("staged"), sem("bias_ready")
        scores_ready, scores_read, exp_ready = sem("scores_ready"), sem("scores_read"), sem("exp_ready")
        total_ready, recip_ready, probs_ready = sem("total_ready"), sem("recip_ready"), sem("probs_ready")
        probs_turned, turned_copied = sem("probs_turned"), sem("turned_copied")
        o_ready, o_hi_ready, o_read = sem("o_ready"), sem("o_hi_ready"), sem("o_read")
        cw_ready, conv_step, gate_ready = sem("cw_ready"), sem("conv_step"), sem("gate_ready")
        hid_f, hid_hi, hid_ready = sem("hid_f"), sem("hid_hi"), sem("hid_ready")
        block_built, block_hi, block_ready = sem("block_built"), sem("block_hi"), sem("block_ready")
        cmp_h_ready, cleared = sem("cmp_h_ready"), sem("cleared")
        wg_hi, wg_ready, kc_done, gate_dot, kc_ready = sem("wg_hi"), sem("wg_ready"), sem("kc_done"), sem("gate_dot"), sem("kc_ready")
        vc_ready, gate_exp, gate_plus, gates_ready = sem("vc_ready"), sem("gate_exp"), sem("gate_plus"), sem("gates_ready")
        passed_dve, passed_pool = sem("passed_dve"), sem("passed_pool")
        out_ready, out_done = sem("out_ready"), sem("out_done")

        N_CONST = 11

        def items_before(layer, g=0):
            return (0 if layer == 0 else GROUPS * HPG) + g * len(attention_items(layer))

        def bias_before(layer):
            return 0 if layer == 0 else HPG + 3 * HPG

        n_bias = [HPG, 2 * HPG]
        n_staged = [4, 7]

        def staged_after(layer, g):
            return (0 if layer == 0 else GROUPS * n_staged[0]) + n_staged[layer] * (g + 1)

        def set_of(u):
            if u in (KV0, KC1, KW1, WV1):
                return 1
            if Q0 <= u <= O0 or Q1 <= u <= O1 or u in (KS1, WK1):
                return 0
            base = next(b for b in (DN1, FF1, O1, DN0, FF0, O0) if u >= b)
            return (u - base) % 2

        def before_in_set(u):
            for v in range(u - 1, -1, -1):
                if set_of(v) == set_of(u):
                    return v
            return None

        block = ctx.enter_context(nc.Block())

        @block.sync
        def _(sp):
            sp.dma_start(xT[:], x).then_inc(x_in, 16)
            for s in range(RING):
                sp.dma_start(raw[:, s, :], stream[s]).then_inc(raw_in[s], 16)
            turns = stream.rearrange("(n s) p c -> n s p c", s=RING)
            with sp.Fori(0, CHUNKS // RING - 1) as n:
                for s in range(RING):
                    sp.wait_ge(lo_ready, n * RING + (s + 1))
                    sp.dma_start(raw[:, s, :], turns[n + 1, s]).then_inc(raw_in[s], 16)
            for q in range(4):
                sp.wait_ge(out_ready, q + 1)
                sp.dma_start(out[:, q * 4:(q + 1) * 4, :], xT[:, q * 4:(q + 1) * 4, :]).then_inc(out_done, 16)
            sp.wait_ge(out_done, 64)

        @block.gpsimd
        def _(pool):
            nc.gpsimd.memset(ones[:], 1.0).then_inc(filled, 1)
            nc.gpsimd.memset(eps[:], EPS).then_inc(filled, 1)
            nc.gpsimd.memset(ident[:], 0.0).then_inc(filled, 1)
            pool.wait_ge(filled, 3)
            nc.gpsimd.affine_select(out=ident[:], in_=ident[:], compare_op=ALU.not_equal, fill=1.0, base=0,
                                    pattern=[[-1, P]], channel_multiplier=1).then_inc(filled, 1)
            pool_sem = [0]
            made = sem("made")

            def step(ins):
                pool_sem[0] += 1
                ins.then_inc(made, 1)
                pool.wait_ge(made, pool_sem[0])

            def causal(t, window):
                step(nc.gpsimd.affine_select(out=t[:, 0:P], in_=t[:, 0:P], compare_op=ALU.is_ge, fill=FAR,
                                             base=0, pattern=[[-1, P]], channel_multiplier=1))
                last = nc.gpsimd.affine_select(out=t[:, P:], in_=t[:, P:], compare_op=ALU.is_ge, fill=FAR,
                                               base=P, pattern=[[-1, S]], channel_multiplier=1)
                if window:
                    step(last)
                    last = nc.gpsimd.affine_select(out=t[:, P:], in_=t[:, P:], compare_op=ALU.is_ge, fill=FAR,
                                                   base=WINDOW - 1 - P, pattern=[[1, S]], channel_multiplier=-1)
                return last

            def bias_tables(layer):
                step(nc.gpsimd.iota(dist[:, 0:P], pattern=[[-1, P]], base=0, channel_multiplier=1,
                                    allow_small_or_imprecise_dtypes=True))
                step(nc.gpsimd.iota(dist[:, P:], pattern=[[-1, S]], base=P, channel_multiplier=1,
                                    allow_small_or_imprecise_dtypes=True))
                for i in range(HPG):
                    slope = float(np.exp2(np.float32(-8.0 * (i + 1) / NH)))
                    step(nc.gpsimd.tensor_scalar(bias[:, i, :], dist[:], slope, 1.0, ALU.mult, ALU.mult))
                    causal(bias[:, i, :], layer == 0).then_inc(bias_ready, 1)
                if layer == 1:
                    step(nc.gpsimd.iota(dist[:, 0:2 * NC].rearrange("p (t n) -> p t n", t=TT),
                                        pattern=[[P, TT], [-CMP_STRIDE, NC]], base=1 - CMP_LEN, channel_multiplier=1,
                                        allow_small_or_imprecise_dtypes=True))
                    for i in range(HPG):
                        slope = float(np.exp2(np.float32(-8.0 * (i + 1) / NH)))
                        step(nc.gpsimd.tensor_scalar(bias_c[:, i, :], dist[:, 0:2 * NC], slope, 1.0, ALU.mult, ALU.mult))
                        t = bias_c[:, i, :].rearrange("p (t n) -> p t n", t=TT)
                        nc.gpsimd.affine_select(out=t, in_=t, compare_op=ALU.is_ge, fill=FAR, base=1 - CMP_LEN,
                                                pattern=[[P, TT], [-CMP_STRIDE, NC]],
                                                channel_multiplier=1).then_inc(bias_ready, 1)

            def stage(layer, g):
                pool.wait_ge(o_ready, items_before(layer, g))
                cp = nc.gpsimd.tensor_copy
                cp(k_g[:, 0, :], k_dup[:, 0, g, :]).then_inc(staged, 1)
                cp(v_g[:, 0, :, :], v_nat[:, 0, :, bass.ds(g * HD, HD)]).then_inc(staged, 1)
                if layer == 0:
                    cp(sinks_g[:], sinks_sb[:, bass.ds(g * HPG, HPG)]).then_inc(staged, 1)
                    cp(neg_sinks_g[:], neg_sinks[:, bass.ds(g * HPG, HPG)]).then_inc(staged, 1)
                    return
                cp(k_g[:, 1, :], k_dup[:, 1, g, :]).then_inc(staged, 1)
                cp(v_g[:, 1, :, :], v_nat[:, 1, :, bass.ds(g * HD, HD)]).then_inc(staged, 1)
                cp(kc_g[:], kc_all[:, bass.ds(g * NC, NC)]).then_inc(staged, 1)
                cp(vc_g[0:NC, :], vc_all[0:NC, bass.ds(g * HD, HD)]).then_inc(staged, 1)
                cp(gates_g[:], gates[:, :, bass.ds(g * 24, 24)]).then_inc(staged, 1)

            for layer in range(2):
                if layer == 1:
                    pool.wait_ge(chunk_used, first_chunk(KC1))
                bias_tables(layer)
                pool.wait_ge(k_dup_ready, 1 if layer == 0 else 3)
                pool.wait_ge(v_ready, 1 if layer == 0 else 3)
                if layer == 0:
                    pool.wait_ge(prepared, 1)
                else:
                    pool.wait_ge(kc_ready, 1)
                    pool.wait_ge(vc_ready, 1)
                    pool.wait_ge(gates_ready, 1)
                stage(layer, 0)
                items = attention_items(layer)
                with pool.Fori(0, GROUPS - 1) as g:
                    for n, (i, kind) in enumerate(items):
                        if kind == "sel":
                            continue
                        pool.wait_ge(scores_read, g * len(items) + (items_before(layer) + n + 1))
                        pool.sem_inc(passed_pool, 1)
                        t = bias_c[:, i, :] if kind == "cmp" else bias[:, i, :]
                        nc.gpsimd.tensor_scalar(t, t, 0.25, 1.0, ALU.mult, ALU.mult).then_inc(bias_ready, 1)
                    stage(layer, g + 1)
                ff = FF0 if layer == 0 else FF1
                pool.wait_ge(chunk_used, first_chunk(ff))
                nc.gpsimd.tensor_copy(cw[:].rearrange("p a b -> p (a b)"), conv_sb[:, layer, 0, :]).then_inc(cw_ready, 1)
                with pool.Fori(1, NF) as f:
                    pool.wait_ge(conv_step, f * 3 + layer * 3 * NF)
                    nc.gpsimd.tensor_copy(cw[:].rearrange("p a b -> p (a b)"),
                                          conv_sb[:, layer, f, :]).then_inc(cw_ready, 1)

        @block.tensor
        def _(pe):
            mm = nc.tensor.matmul

            def chunk(c, last_c, g, slot, u, rhs, width, kt0, at, tile_before=None):
                w = width
                for t in range(UT):
                    if tile_before:
                        tile_before(c * UT + t)
                    if c == 0 and at is not None:
                        pe.wait_ge(evacuated, at + t)
                    if t == 0:
                        pe.wait_ge(lo_ready, g + 1)
                    bank = sets[set_of(u)][:, t, :]
                    for j in range(CK):
                        cols = slice(j * UNIT + t * P, j * UNIT + (t + 1) * P)
                        first, final = c == 0 and j == 0, c == last_c and j == CK - 1
                        r = rhs(kt0 + j)

                        def high():
                            return mm(bank[:, 0:2 * w], whi[:, slot, cols], r, start=first, stop=final)

                        def low():
                            return mm(bank[:, w:2 * w], wlo[:, slot, cols], r[:, 0:w], start=False, stop=False)

                        if final:
                            low()
                            last = high()
                        else:
                            high()
                            last = low()
                last.then_inc(chunk_used, 1)

            def unit(u, source, lp=None, width=S, waits=None, tile_before=None, after_chunk=None):
                n = CHF if source is hid else CH
                v = before_in_set(u)
                more_g, more_e = (lp[0] * lp[1], lp[0] * lp[2]) if lp else (0, 0)
                at = None if v is None else more_e + (UT * v + 1)
                for c in range(n):
                    g0 = first_chunk(u) + c
                    if waits:
                        waits(c)
                    chunk(c, n - 1, more_g + g0, g0 % RING, u, lambda kt: source[:, kt, :], width, CK * c, at,
                          tile_before)
                    if after_chunk:
                        after_chunk(c)

            def mean_of_squares(tile, n, ready, first, last, bank):
                for t in range(n):
                    ins = mm(ps_mean[bank], ones[:], tile[:, t, :], start=first and t == 0, stop=last and t == n - 1)
                return ins

            def prenorm(n):
                if n == 0:
                    pe.wait_ge(filled, 4)
                for q in range(4):
                    pe.wait_ge(sq_ready, 4 * n + q + 1)
                    ins = mean_of_squares(squares[:, q % 2], UT, None, q == 0, q == 3, 1)
                    ins.then_inc(sq_used if q < 3 else mean_ready, 1)

            def postnorm(n):
                pe.wait_ge(sq_sum_ready, 4 * n + 4)
                mean_of_squares(sq_sum, UT, None, True, True, 0).then_inc(mean_ready, 1)

            def h_waits(n):
                return lambda c: pe.wait_ge(h_ready, 4 * n + (CK * c) // 4 + 1)

            def attention(layer, u_q, g, last):
                items = attention_items(layer)
                ib = items_before(layer) + g * len(items)
                pairs = 16 * layer + 4 * g
                at = attention_slots(layer, last)

                def scores(s):
                    i, kind = items[s]
                    hp = slice((i % 2) * HD, (i % 2) * HD + HD)
                    if s == 0:
                        pe.wait_ge(evacuated, u_q)
                        pe.wait_ge(staged, staged_after(layer, g))
                    if s >= 2:
                        pe.wait_ge(scores_read, ib + (s - 1))
                    q = qg[hp, i // 2, :]
                    b = ps_scores[s % 2]
                    if kind == "cmp":
                        mm(b[:, 0:NC], q[:, 0:P], kc_g[hp, :], start=True, stop=True)
                        ins = mm(b[:, NC:2 * NC], q[:, P:S], kc_g[hp, :], start=True, stop=True)
                    else:
                        k = k_g[hp, 1 if kind == "win" else 0, :]
                        mm(b[:, 0:P], q[:, 0:P], k[:, 0:P], start=True, stop=True)
                        ins = mm(b[:, P:CAUSAL], q[:, P:S], k, start=True, stop=True)
                    ins.then_inc(scores_ready, 1)

                def turn(s):
                    kind = items[s][1]
                    pe.wait_ge(probs_ready, ib + (s + 1))
                    if s >= 1:
                        pe.wait_ge(turned_copied, ib + s)
                    e = probs[:, s % LAG, :]
                    if kind == "cmp":
                        for t in range(TT):
                            ins = nc.tensor.transpose(ps_turned[0:NC, t * P:(t + 1) * P], e[:, t * NC:(t + 1) * NC],
                                                      ident[:])
                    else:
                        for t in range(3):
                            ins = nc.tensor.transpose(ps_turned[:, t * P:(t + 1) * P], e[:, t * P:(t + 1) * P], ident[:])
                    ins.then_inc(probs_turned, 1)

                def outputs(s):
                    i, kind = items[s]
                    hp = slice((i % 2) * HD, (i % 2) * HD + HD)
                    first = kind in ("swa", "sel")
                    pe.wait_ge(turned_copied, ib + (s + 1))
                    if first and i % 2 == 0:
                        pe.wait_ge(o_read, 1 + pairs + i // 2)
                    e = turned[:, s % 2, :]
                    if kind == "cmp":
                        ins = mm(ps_o[hp, 0:S], vc_g[0:NC, :], e[0:NC, 0:S], start=False, stop=True)
                    else:
                        v = v_g[:, 1 if kind == "win" else 0]
                        mm(ps_o[hp, 0:S], v[:, 0, :], e[:, 0:S], start=first, stop=False)
                        ins = mm(ps_o[hp, P:S], v[:, 1, :], e[:, S:CAUSAL], start=False, stop=kind == "swa")
                    ins.then_inc(o_ready, 1)

                def before(tile):
                    for s in at[tile]:
                        if LAG <= s < len(items) + LAG:
                            turn(s - LAG)
                        if s < len(items):
                            scores(s)
                        if LAG + 1 <= s < len(items) + LAG + 1:
                            outputs(s - LAG - 1)

                return before

            def turn_values(which, b):
                for tt in range(TT):
                    for f in range(2):
                        ins = nc.tensor.transpose(sets[1][:, b, tt * S + f * P:tt * S + (f + 1) * P],
                                                  v_raw[:, which, f, tt * P:(tt + 1) * P], ident[:])
                ins.then_inc(v_turned, 1)

            def after_q0(layer):
                def after(c):
                    if c != 5:
                        return
                    if layer == 0:
                        pe.wait_ge(evacuated, UT * (KV0 + 1))
                        turn_values(0, 0)
                        return
                    pe.wait_ge(evacuated, UT * (WV1 + 1))
                    turn_values(0, 0)
                    turn_values(1, 1)
                    pe.wait_ge(cmp_h_ready, 2)
                    pe.wait_ge(late_in, 16 * 4)
                    for t in range(UT):
                        ins = mm(ps_turned[:, 0:GROUPS * NC], w2k_sb[:, t, :], cmp_h[:, 0, t, :],
                                 start=t == 0, stop=t == UT - 1)
                    ins.then_inc(kc_done, 1)
                    for g in range(GROUPS):
                        o = ps_o[0:NC, g * HD:(g + 1) * HD]
                        for t in range(UT):
                            mm(o, cmp_h[:, 1, t, g * NC:(g + 1) * NC], w2v_sb[:, t, :], start=t == 0, stop=False)
                        ins = mm(o, ones[0:1, 0:NC], b2v_sb[0:1, :], start=False, stop=True)
                    pe.wait_ge(wg_ready, 1)
                    for tt in range(TT):
                        o = ps_o[:, S + tt * 96:S + (tt + 1) * 96]
                        for kt in range(KT):
                            hi = hs[:, kt, tt * P:(tt + 1) * P]
                            lo = hs[:, kt, S + tt * P:S + (tt + 1) * P]
                            mm(o, lo, wg_split[:, kt, 0, :], start=kt == 0, stop=False)
                            mm(o, hi, wg_split[:, kt, 1, :], start=False, stop=False)
                            ins = mm(o, hi, wg_split[:, kt, 0, :], start=False, stop=kt == KT - 1)
                    ins.then_inc(gate_dot, 1)
                return after

            for layer in range(2):
                q0, o0, ff, dn = ((Q0, O0, FF0, DN0), (Q1, O1, FF1, DN1))[layer]
                prenorm(2 * layer)
                hw = h_waits(2 * layer)
                if layer == 0:
                    unit(KV0, hs, waits=hw)
                else:
                    for u in (KC1, KS1, KW1):
                        unit(u, hs, waits=hw)
                    for n, u in enumerate((WK1, WV1)):
                        pe.wait_ge(block_ready, n + 1)
                        unit(u, blocks[n][:].rearrange("p k a b -> p k (a b)"), width=GROUPS * NC)
                unit(q0, hs, after_chunk=after_q0(layer))
                if layer == 1:
                    pe.wait_ge(kc_ready, 1)
                    pe.wait_ge(vc_ready, 1)
                    pe.wait_ge(gate_exp, 1)
                pe.wait_ge(v_ready, 1 if layer == 0 else 3)
                with pe.Fori(0, GROUPS - 1) as g:
                    unit(q0 + 1, hs, lp=(g, CH, UT), tile_before=attention(layer, g * UT + UT * (q0 + 1), g, False))

                def o_waits(c):
                    if c >= 6:
                        pe.wait_ge(o_read, 1 + 16 * layer + CK * c + 2)
                    elif c == 0:
                        pe.wait_ge(o_read, 1 + 16 * layer + 12)

                g = GROUPS - 1
                unit(o0, os_, waits=o_waits, tile_before=attention(layer, UT * (q0 + g + 1), g, True))
                for u in range(o0 + 1, o0 + 4):
                    unit(u, os_)
                postnorm(2 * layer)
                prenorm(2 * layer + 1)
                hw = h_waits(2 * layer + 1)
                with pe.Fori(0, NF) as f:
                    for u in (ff, ff + 1):
                        unit(u, hs, lp=(f, 2 * CH, 2 * UT), waits=hw if u == ff else None)

                def hid_waits(c):
                    if c % 2 == 0 and c // 2 >= NF - 2:
                        pe.wait_ge(hid_ready, NF * layer + c // 2 + 1)
                    elif c == 0:
                        pe.wait_ge(hid_ready, NF * layer + NF - 2)

                if layer == 0:
                    with pe.Fori(0, 2) as i:
                        for u in (dn, dn + 1):
                            unit(u, hid, lp=(i, 2 * CHF, 2 * UT), waits=hid_waits if u == dn else None)
                else:
                    for u in range(dn, dn + 4):
                        unit(u, hid, waits=hid_waits if u == dn else None)
                postnorm(2 * layer + 1)

        @block.scalar
        def _(act):
            A = nc.scalar.activation
            consts = ((g_sb, gains), (conv_sb, conv), (b_in_sb, b_in), (b_o_sb, b_o),
                      (sinks_sb, sinks.partition_broadcast(P)), (b1_sb, b1))
            for dst, src in consts:
                act.dma_start(dst[:], src).then_inc(const_in, 16)
            for h in range(2):
                half_p = slice(h * HD, (h + 1) * HD)
                act.dma_start(pe_sb[half_p], pe).then_inc(const_in, 16)
                act.dma_start(b2k_sb[half_p, :], b2k).then_inc(const_in, 16)
            act.dma_start(b2v_sb[0:1, :], b2v).then_inc(const_in, 16)

            def split(g0, more=0, turn=0):
                slot = g0 % RING
                act.wait_ge(raw_in[slot], turn + 16 * (g0 // RING + 1))
                if g0 >= RING:
                    act.wait_ge(chunk_used, more + (g0 - RING + 1))
                A(whi[:, slot, :], raw[:, slot, :], ACT.Copy).then_inc(hi_ready, 1)

            def loop_terms(lp):
                return (lp[0] * lp[1], lp[0] * (lp[1] // RING * 16), lp[0] * lp[2]) if lp else (0, 0, 0)

            def unit_first_half(u, lp=None, bias_of=None, scale=1.0, width=S):
                more, _, more_e = loop_terms(lp)
                n = CHF if (DN0 <= u < DN0 + 4 or u >= DN1) else CH
                act.wait_ge(chunk_used, more + (first_chunk(u) + n))
                st = set_of(u)
                if bias_of is None:
                    if scale == 1.0:
                        A(half[:, st, :, 0:width], sets[st][:, :, 0:width], ACT.Copy).then_inc(half_ready, UT)
                    else:
                        for t in range(UT):
                            A(half[:, st, t, :], sets[st][:, t, 0:S], ACT.Copy, scale=scale).then_inc(half_ready, 1)
                else:
                    for t in range(UT):
                        A(half[:, st, t, :], sets[st][:, t, 0:S], ACT.Identity, bias=bias_of(t),
                          scale=scale).then_inc(half_ready, 1)

            def unit(u, evac, lp=None, tail=True):
                more, turn, _ = loop_terms(lp)
                n = CHF if (DN0 <= u < DN0 + 4 or u >= DN1) else CH
                g0 = first_chunk(u)
                last = u == UNITS - 1
                for c in range(RING, n + (0 if last else RING - 1)):
                    split(g0 + c, more, turn)
                evac()
                if not last:
                    split(g0 + n + RING - 1, more, turn)

            def finish_norm(bank, k):
                act.wait_ge(mean_ready, k + 1)
                A(root[:], ps_mean[bank], ACT.Sqrt, bias=eps[:], scale=1.0 / D).then_inc(root_ready, 1)

            def prenorm(n):
                for q in range(4):
                    if n == 0:
                        act.wait_ge(x_in, 16)
                    else:
                        act.wait_ge(x_ready, 4 * (n - 1) + q + 1)
                    if q >= 2:
                        act.wait_ge(sq_used, 3 * n + q - 1)
                    A(squares[:, q % 2], xT[:, q * 4:(q + 1) * 4, :], ACT.Square).then_inc(sq_ready, 1)
                if n == 0:
                    act.wait_ge(filled, 4)
                finish_norm(1, 2 * n)
                for q in range(4):
                    act.wait_ge(hf_ready, 4 * n + q + 1)
                    A(hs[:, q * 4:(q + 1) * 4, 0:S], half[:, q % 2], ACT.Copy).then_inc(h_hi_ready, 1)

            def y_evac(u, base, k, lp=None, bias_of=None):
                def evac():
                    unit_first_half(u, lp, bias_of)
                    st = set_of(u)
                    i, per = (lp[0], 2) if lp else (0, 0)
                    more_e = lp[0] * lp[2] if lp else 0
                    act.wait_ge(evacuated, more_e + UT * (u + 1))
                    if base + k >= 2:
                        act.wait_ge(sq_sum_ready, i * per + (base + k - 1))
                    A(squares[:, k % 2], y[:, bass.ds(i * (per * UT) + k * UT, UT), :], ACT.Square).then_inc(y_sq_ready, 1)
                return evac

            def attention(layer, g, last):
                items = attention_items(layer)
                ib = items_before(layer) + g * len(items)
                pairs = 16 * layer + 4 * g
                at = attention_slots(layer, last)

                def copy_turned(s):
                    act.wait_ge(probs_turned, ib + (s + 1))
                    if s >= 2:
                        act.wait_ge(o_ready, ib + (s - 1))
                    if items[s][1] == "cmp":
                        A(turned[0:NC, s % 2, 0:S], ps_turned[0:NC, 0:S], ACT.Copy).then_inc(turned_copied, 1)
                    else:
                        A(turned[:, s % 2, :], ps_turned[:, 0:CAUSAL], ACT.Copy).then_inc(turned_copied, 1)

                def exponents(s):
                    i, kind = items[s]
                    act.wait_ge(scores_read, ib + (s + 1))
                    b = s % 2
                    ends = (0, NC, 2 * NC) if kind == "cmp" else (0, P, CAUSAL)
                    for t in range(TT):
                        cols = slice(ends[t], ends[t + 1])
                        ins = A(probs[:, s % LAG, cols], scored[:, b, cols], ACT.Exp, bias=neg_max[:, b, t:t + 1],
                                scale=-1.0, accum_out=sums[:, b, t:t + 1])
                    if kind == "swa":
                        ins = A(sink_e[:, b, :], neg_max[:, b, :], ACT.Exp, bias=sinks_g[:, i:i + 1])
                    ins.then_inc(exp_ready, 1)

                def pair_high(s):
                    p = items[s][0] // 2
                    act.wait_ge(o_ready, ib + (s + 1))
                    A(os_[:, bass.ds(g * 4 + p, 1), 0:S].rearrange("p a b -> p (a b)"), ps_o[:, 0:S],
                      ACT.Copy).then_inc(o_hi_ready, 1)

                def step(tile):
                    for s in at[tile]:
                        if s == 0:
                            act.wait_ge(staged, staged_after(layer, g))
                        if LAG <= s < len(items) + LAG:
                            copy_turned(s - LAG)
                        o = s - LAG - 2
                        if o >= 0 and items[o][0] % 2 == 1 and items[o][1] in ("swa", "cmp"):
                            pair_high(o)
                        if s < len(items):
                            exponents(s)

                return step

            def attention_unit(u, evac, step, lp=None):
                more, turn, _ = loop_terms(lp)
                g0 = first_chunk(u)
                for tile in range(CH * UT):
                    step(tile)
                    if tile >= UT and tile % UT == 0:
                        split(g0 + RING + tile // UT - 1, more, turn)
                evac()
                split(g0 + CH + RING - 1, more, turn)

            for g in range(RING):
                split(g)
            act.wait_ge(const_in, 16 * N_CONST)
            for layer in range(2):
                q0, o0, ff, dn = ((Q0, O0, FF0, DN0), (Q1, O1, FF1, DN1))[layer]
                if layer == 1:
                    act.wait_ge(chunk_used, first_chunk(KC1))
                    act.dma_start(wg_raw[:], w_gates).then_inc(late_in, 16)
                    act.dma_start(w2k_sb[:, :, 0:HD], w2[:, 0]).then_inc(late_in, 16)
                    act.dma_start(w2k_sb[:, :, HD:P], w2[:, 0]).then_inc(late_in, 16)
                    act.dma_start(w2v_sb[:], w2[:, 1]).then_inc(late_in, 16)
                prenorm(2 * layer)
                if layer == 0:
                    unit(KV0, lambda: unit_first_half(KV0, bias_of=lambda t: b_in_sb[:, 16 + t:17 + t]))
                else:
                    unit(KC1, lambda: unit_first_half(KC1))
                    act.wait_ge(late_in, 64)
                    A(wg_split[:, :, 0, :], wg_raw[:], ACT.Copy).then_inc(wg_hi, 1)
                    for n, u in enumerate((KS1, KW1)):
                        unit(u, lambda u=u: unit_first_half(u))
                        act.wait_ge(block_built, n + 1)
                        A(blocks[n][:, :, 0, :], block_f[:], ACT.Copy).then_inc(block_hi, 1)
                    for n, u in enumerate((WK1, WV1)):
                        def evac(u=u, n=n):
                            unit_first_half(u, width=GROUPS * NC)
                            act.wait_ge(evacuated, UT * (u + 1))
                            A(cmp_h[:, n], cmp_z[:], ACT.Gelu_apprx_tanh).then_inc(cmp_h_ready, 1)
                        unit(u, evac)

                def after_values():
                    if layer == 0:
                        act.wait_ge(v_turned, 1)
                        A(v_nat[:, 0].rearrange("p a b -> p (a b)"), sets[1][:, 0, :], ACT.Copy).then_inc(v_ready, 1)
                        return
                    for w in range(2):
                        act.wait_ge(v_turned, 2 + w)
                        A(v_nat[:, w].rearrange("p a b -> p (a b)"), sets[1][:, w, :], ACT.Copy).then_inc(v_ready, 1)
                    act.wait_ge(kc_done, 1)
                    A(kc_all[:], ps_turned[:, 0:GROUPS * NC], ACT.Identity, bias=b2k_sb[:]).then_inc(kc_ready, 1)
                    act.wait_ge(gate_dot, 1)
                    A(vc_all[0:NC, :], ps_o[0:NC, 0:S], ACT.Copy).then_inc(vc_ready, 1)
                    A(gates[:].rearrange("p a b -> p (a b)"), ps_o[:, S:S + TT * 96], ACT.Exp,
                      scale=-1.0).then_inc(gate_exp, 1)

                def q_evac(u, lp=None):
                    if layer == 1:
                        return lambda: unit_first_half(u, lp, scale=-HD ** -0.5)
                    if lp is None:
                        return lambda: unit_first_half(u, lp, scale=-HD ** -0.5, bias_of=lambda t: b_q[:, t:t + 1])
                    return lambda: unit_first_half(
                        u, lp, scale=-HD ** -0.5, bias_of=lambda t: b_q[:, bass.ds(lp[0] * UT + (UT + t), 1)])

                if layer == 0:
                    act.wait_ge(prepared, 1)

                def q0_evac():
                    after_values()
                    q_evac(q0)()

                unit(q0, q0_evac)
                with act.Fori(0, GROUPS - 1) as g:
                    lp = (g, CH, UT)
                    attention_unit(q0 + 1, q_evac(q0 + 1, lp), attention(layer, g, False), lp)
                bias_of = (lambda k: lambda t: b_o_sb[:, k * UT + t:k * UT + t + 1]) if layer == 0 else lambda k: None
                base = 8 * layer
                attention_unit(o0, y_evac(o0, base, 0, None, bias_of(0)), attention(layer, GROUPS - 1, True))
                for k in range(1, 4):
                    unit(o0 + k, y_evac(o0 + k, base, k, None, bias_of(k)))
                finish_norm(0, 4 * layer + 1)
                prenorm(2 * layer + 1)
                with act.Fori(0, NF) as f:
                    lp = (f, 2 * CH, 2 * UT)
                    more, turn, _ = loop_terms(lp)
                    unit(ff, lambda: unit_first_half(ff, lp), lp)
                    g0 = first_chunk(ff + 1)
                    for c in range(RING, CH):
                        split(g0 + c, more, turn)
                    act.wait_ge(conv_step, f * 3 + (3 * NF * layer + 3))
                    A(gate[:], gate[:], ACT.Silu).then_inc(gate_ready, 1)
                    for c in range(CH, CH + RING - 1):
                        split(g0 + c, more, turn)
                    unit_first_half(ff + 1, lp)
                    split(g0 + CH + RING - 1, more, turn)
                    act.wait_ge(hid_f, f + (NF * layer + 1))
                    A(hid[:, bass.ds(f * UT, UT), 0:S], gate[:], ACT.Copy).then_inc(hid_hi, 1)
                if layer == 0:
                    with act.Fori(0, 2) as i:
                        lp = (i, 2 * CHF, 2 * UT)
                        for k in range(2):
                            unit(dn + k, y_evac(dn + k, base + 4, k, lp), lp)
                else:
                    for k in range(4):
                        unit(dn + k, y_evac(dn + k, base + 4, k))
                finish_norm(0, 4 * layer + 3)

        @block.vector
        def _(dve):
            V = nc.vector
            dve.wait_ge(const_in, 16 * N_CONST)
            V.tensor_scalar(b_q[:], b_in_sb[:, 0:16], -HD ** -0.5, None, ALU.mult).then_inc(o_read, 1)
            V.tensor_scalar(neg_sinks[:], sinks_sb[:], -1.0, None, ALU.mult).then_inc(prepared, 1)

            def split(g0, more=0):
                slot = g0 % RING
                dve.wait_ge(hi_ready, more + (g0 + 1))
                V.tensor_tensor(wlo[:, slot, :], raw[:, slot, :], whi[:, slot, :].bitcast(F32),
                                ALU.subtract).then_inc(lo_ready, 1)

            def loop_terms(lp):
                return (lp[0] * lp[1], lp[0] * lp[2]) if lp else (0, 0)

            def unit(u, evac, lp=None):
                more, _ = loop_terms(lp)
                n = CHF if (DN0 <= u < DN0 + 4 or u >= DN1) else CH
                g0 = first_chunk(u)
                last = u == UNITS - 1
                for c in range(RING, n + (0 if last else RING - 1)):
                    split(g0 + c, more)
                evac()
                if not last:
                    split(g0 + n + RING - 1, more)

            def add_halves(u, dst, lp=None, scale=None, width=S):
                _, more_e = loop_terms(lp)
                st = set_of(u)
                for t in range(UT):
                    dve.wait_ge(half_ready, more_e + (UT * u + t + 1))
                    b, h = sets[st][:, t, width:2 * width], half[:, st, t, 0:width]
                    if scale is None:
                        ins = V.tensor_tensor(dst(t), h, b, ALU.add)
                    else:
                        ins = V.scalar_tensor_tensor(dst(t), b, scale, h, ALU.mult, ALU.add)
                    ins.then_inc(evacuated, 1)

            def finish_norm(k):
                dve.wait_ge(root_ready, k + 1)
                V.reciprocal(rnorm[:], root[:]).then_inc(rnorm_ready, 1)
                dve.wait_ge(rnorm_ready, k + 1)

            def prenorm(n, gain):
                finish_norm(2 * n)

                def scaled(q):
                    for t in range(UT):
                        ins = V.scalar_tensor_tensor(half[:, q % 2, t, :], xT[:, q * 4 + t, :],
                                                     g_sb[:, gain, q * 4 + t:q * 4 + t + 1], rnorm[:], ALU.mult, ALU.mult)
                    ins.then_inc(hf_ready, 1)

                def low(q):
                    dve.wait_ge(h_hi_ready, 4 * n + q + 1)
                    V.tensor_tensor(hs[:, q * 4:(q + 1) * 4, S:2 * S], half[:, q % 2],
                                    hs[:, q * 4:(q + 1) * 4, 0:S].bitcast(F32), ALU.subtract).then_inc(h_ready, 1)

                scaled(0)
                scaled(1)
                for q in range(4):
                    low(q)
                    if q + 2 < 4:
                        dve.wait_ge(h_ready, 4 * n + q + 1)
                        scaled(q + 2)

            def postnorm(n, gain, last=False):
                finish_norm(2 * n + 1)
                for q in range(4):
                    for t in range(UT):
                        kt = q * 4 + t
                        ins = V.scalar_tensor_tensor(y[:, kt, :], y[:, kt, :], g_sb[:, gain, kt:kt + 1], rnorm[:],
                                                     ALU.mult, ALU.mult)
                    ins.then_inc(y_scaled, 1)
                    dve.wait_ge(y_scaled, 4 * n + q + 1)
                    V.tensor_tensor(xT[:, q * 4:(q + 1) * 4, :], xT[:, q * 4:(q + 1) * 4, :], y[:, q * 4:(q + 1) * 4, :],
                                    ALU.add).then_inc(out_ready if last else x_ready, 1)

            def y_evac(u, base, k, lp=None):
                def evac():
                    i, per = (lp[0], 2) if lp else (0, 0)
                    add_halves(u, lambda t: y[:, bass.ds(i * (per * UT) + (k * UT + t), 1), :].rearrange("p a b -> p (a b)"), lp)
                    dve.wait_ge(y_sq_ready, i * per + (base + k + 1))
                    if lp is not None and k == 0:
                        dve.wait_ge(sq_sum_ready, i * per + (base + k))
                        V.tensor_tensor(sq_sum[:], sq_sum[:], squares[:, k % 2], ALU.add).then_inc(sq_sum_ready, 1)
                    elif k == 0:
                        V.tensor_copy(sq_sum[:], squares[:, k % 2]).then_inc(sq_sum_ready, 1)
                    else:
                        dve.wait_ge(sq_sum_ready, i * per + (base + k))
                        V.tensor_tensor(sq_sum[:], sq_sum[:], squares[:, k % 2], ALU.add).then_inc(sq_sum_ready, 1)
                return evac

            def attention(layer, g, last):
                items = attention_items(layer)
                ib = items_before(layer) + g * len(items)
                at = attention_slots(layer, last)
                tb = 8 * GROUPS * layer + g * HPG

                def add_bias(s):
                    i, kind = items[s]
                    b = s % 2
                    dve.wait_ge(scores_ready, ib + (s + 1))
                    if s == 0:
                        dve.wait_ge(bias_ready, bias_before(layer) + n_bias[layer] * (g + 1))
                        dve.wait_ge(staged, staged_after(layer, g))
                    dve.sem_inc(passed_dve, 1)
                    ends = (0, NC, 2 * NC) if kind == "cmp" else (0, P, CAUSAL)
                    table = bias_c if kind == "cmp" else bias
                    for t in range(TT):
                        cols = slice(ends[t], ends[t + 1])
                        ins = V.tensor_tensor_reduce(
                            out=scored[:, b, cols], in0=ps_scores[b][:, cols], in1=table[:, i, cols], scale=1.0,
                            scalar=neg_sinks_g[:, i:i + 1] if kind == "swa" else NO_KEY,
                            op0=ALU.add, op1=ALU.min, accum_out=neg_max[:, b, t:t + 1])
                    ins.then_inc(scores_read, 1)

                def normalize(s):
                    i, kind = items[s]
                    b = s % 2
                    dve.wait_ge(exp_ready, ib + (s + 1))
                    tot = sums
                    if kind == "swa":
                        V.tensor_tensor(total[:, b, :], sums[:, b, :], sink_e[:, b, :], ALU.add).then_inc(total_ready, 1)
                    elif kind == "cmp":
                        V.tensor_scalar(total[:, b, :], sums[:, b, :], 1e-30, None, ALU.max).then_inc(total_ready, 1)
                    if kind in ("swa", "cmp"):
                        tot = total
                        dve.wait_ge(total_ready, tb + (i + 1))
                    V.reciprocal(recip[:, b, :], tot[:, b, :]).then_inc(recip_ready, 1)
                    dve.wait_ge(recip_ready, ib + (s + 1))
                    ends = (0, NC, 2 * NC) if kind == "cmp" else (0, P, CAUSAL)
                    which = {"cmp": 0, "sel": 1, "win": 2}
                    for t in range(TT):
                        e = probs[:, s % LAG, ends[t]:ends[t + 1]]
                        r = recip[:, b, t:t + 1]
                        if kind == "swa":
                            ins = V.tensor_scalar(e, e, r, None, ALU.mult)
                        else:
                            c = 3 * i + which[kind]
                            ins = V.tensor_scalar(e, e, r, gates_g[:, t, c:c + 1], ALU.mult, ALU.mult)
                    ins.then_inc(probs_ready, 1)

                def pair_low(s):
                    p = items[s][0] // 2
                    dve.wait_ge(o_hi_ready, 16 * layer + 4 * g + (p + 1))
                    at_pair = os_[:, bass.ds(g * 4 + p, 1), :].rearrange("p a b -> p (a b)")
                    V.tensor_tensor(at_pair[:, S:2 * S], ps_o[:, 0:S], at_pair[:, 0:S].bitcast(F32),
                                    ALU.subtract).then_inc(o_read, 1)

                def step(tile):
                    for s in at[tile]:
                        o = s - LAG - 2
                        if o >= 0 and items[o][0] % 2 == 1 and items[o][1] in ("swa", "cmp"):
                            pair_low(o)
                        if s < len(items):
                            add_bias(s)
                        if 1 <= s < len(items) + 1:
                            normalize(s - 1)

                return step

            def attention_unit(u, evac, step, lp=None):
                more, _ = loop_terms(lp)
                g0 = first_chunk(u)
                for tile in range(CH * UT):
                    step(tile)
                    if tile >= UT and tile % UT == 1:
                        split(g0 + RING + tile // UT - 1, more)
                evac()
                split(g0 + CH + RING - 1, more)

            def duplicate(which):
                for j in range(GROUPS):
                    src = k_raw[(j % 2) * HD:(j % 2) * HD + HD, which, j // 2, :]
                    for h in range(2):
                        ins = V.tensor_copy(k_dup[h * HD:(h + 1) * HD, which, j, :], src)
                ins.then_inc(k_dup_ready, 1)

            def build_blocks(n):
                for j in range(GROUPS):
                    hp = (j % 2) * HD
                    for par in range(2):
                        a = kc_raw[hp:hp + HD, n, j // 2, par:par + 1]
                        kv = bass.AP(tensor=a.tensor, offset=a.offset, ap=[a.ap[0], [2, KT], [CMP_STRIDE, NC]])
                        emb = pe_sb[hp:hp + HD, n, par:CMP_LEN:2].unsqueeze(2).to_broadcast([HD, KT, NC])
                        ins = V.tensor_tensor(block_f[par * HD:(par + 1) * HD, :, j * NC:(j + 1) * NC], kv, emb, ALU.add)
                ins.then_inc(block_built, 1)

            for g in range(RING):
                split(g)
            for layer in range(2):
                q0, o0, ff, dn = ((Q0, O0, FF0, DN0), (Q1, O1, FF1, DN1))[layer]
                if layer == 0:
                    dve.wait_ge(x_in, 16)
                prenorm(2 * layer, 4 * layer)
                if layer == 0:
                    unit(KV0, lambda: add_halves(KV0, lambda t: (k_raw if t < 2 else v_raw)[:, 0, t % 2, :]))
                    dve.wait_ge(evacuated, UT * (KV0 + 1))
                    duplicate(0)
                else:
                    unit(KC1, lambda: add_halves(KC1, lambda t: kc_raw[:, t // 2, t % 2, :]))
                    dve.wait_ge(evacuated, UT * (KC1 + 1))
                    build_blocks(0)
                    dve.wait_ge(wg_hi, 1)
                    V.tensor_tensor(wg_split[:, :, 1, :], wg_raw[:], wg_split[:, :, 0, :].bitcast(F32),
                                    ALU.subtract).then_inc(wg_ready, 1)
                    for n, u in enumerate((KS1, KW1)):
                        unit(u, lambda: add_halves(u, lambda t: (k_raw if t < 2 else v_raw)[:, n, t % 2, :]))
                        dve.wait_ge(evacuated, UT * (u + 1))
                        duplicate(n)
                        dve.wait_ge(block_hi, n + 1)
                        V.tensor_tensor(blocks[n][:, :, 1, :], block_f[:], blocks[n][:, :, 0, :].bitcast(F32),
                                        ALU.subtract).then_inc(block_ready, 1)
                        if n == 0:
                            dve.wait_ge(block_ready, 1)
                            build_blocks(1)
                    for n, u in enumerate((WK1, WV1)):
                        w = GROUPS * NC

                        def evac():
                            for t in range(UT):
                                dve.wait_ge(half_ready, UT * (u + 1))
                                if n and t == 0:
                                    dve.wait_ge(cmp_h_ready, 1)
                                st = set_of(u)
                                V.scalar_tensor_tensor(cmp_z[:, t, :], sets[st][:, t, w:2 * w], b1_sb[:, n, t:t + 1],
                                                       half[:, st, t, 0:w], ALU.add, ALU.add).then_inc(evacuated, 1)
                        unit(u, evac)

                def q_dst(t):
                    return qg[:, t, :]

                def q0_evac():
                    if layer == 1:
                        dve.wait_ge(gate_exp, 1)
                        V.tensor_scalar(gates[:], gates[:], 1.0, None, ALU.add).then_inc(gate_plus, 1)
                        dve.wait_ge(gate_plus, 1)
                        V.reciprocal(gates[:], gates[:]).then_inc(gates_ready, 1)
                    add_halves(q0, q_dst, scale=-HD ** -0.5)

                unit(q0, q0_evac)
                with dve.Fori(0, GROUPS - 1) as g:
                    lp = (g, CH, UT)
                    attention_unit(q0 + 1, lambda: add_halves(q0 + 1, q_dst, lp, scale=-HD ** -0.5),
                                   attention(layer, g, False), lp)
                base = 8 * layer
                attention_unit(o0, y_evac(o0, base, 0), attention(layer, GROUPS - 1, True))
                for k in range(1, 4):
                    unit(o0 + k, y_evac(o0 + k, base, k))
                dve.wait_ge(evacuated, UT * (o0 + 4))
                postnorm(2 * layer, 4 * layer + 1)
                dve.wait_ge(x_ready, 4 * (2 * layer + 1))
                prenorm(2 * layer + 1, 4 * layer + 2)

                V.memset(gate_in[:, :, 0:2], 0.0).then_inc(cleared, 1)
                dve.wait_ge(cleared, 1 + 2 * layer)
                with dve.Fori(0, NF) as f:
                    lp = (f, 2 * CH, 2 * UT)
                    more, _ = loop_terms(lp)
                    steps = f * 3 + 3 * NF * layer
                    unit(ff, lambda: add_halves(ff, lambda t: gate_in[:, t, 2:], lp), lp)
                    dve.wait_ge(evacuated, f * (2 * UT) + UT * (ff + 1))
                    dve.wait_ge(cw_ready, f + (NF * layer + 1))
                    for t in range(UT):
                        ins = V.tensor_scalar(gate[:, t, :], gate_in[:, t, 2:], cw[:, t, 2:3], cw[:, t, 3:4],
                                              ALU.mult, ALU.add)
                    ins.then_inc(conv_step, 1)
                    for w in (1, 0):
                        dve.wait_ge(conv_step, steps + (2 - w))
                        for t in range(UT):
                            ins = V.scalar_tensor_tensor(gate[:, t, :], gate_in[:, t, w:w + S], cw[:, t, w:w + 1],
                                                         gate[:, t, :], ALU.mult, ALU.add)
                        ins.then_inc(conv_step, 1)
                    g0 = first_chunk(ff + 1)
                    for c in range(RING, CH + RING - 1):
                        split(g0 + c, more)
                    up = gate_in
                    dve.wait_ge(conv_step, steps + 3)
                    add_halves(ff + 1, lambda t: up[:, t, 2:], lp)
                    split(g0 + CH + RING - 1, more)
                    dve.wait_ge(evacuated, f * (2 * UT) + UT * (ff + 2))
                    dve.wait_ge(gate_ready, f + (NF * layer + 1))
                    V.tensor_tensor(gate[:], gate[:], up[:, :, 2:], ALU.mult).then_inc(hid_f, 1)
                    dve.wait_ge(hid_hi, f + (NF * layer + 1))
                    V.tensor_tensor(hid[:, bass.ds(f * UT, UT), S:2 * S], gate[:],
                                    hid[:, bass.ds(f * UT, UT), 0:S].bitcast(F32), ALU.subtract).then_inc(hid_ready, 1)
                if layer == 0:
                    V.memset(sq_sum[:], 0.0).then_inc(cleared, 1)
                    dve.wait_ge(cleared, 2)
                    with dve.Fori(0, 2) as i:
                        lp = (i, 2 * CHF, 2 * UT)
                        for k in range(2):
                            unit(dn + k, y_evac(dn + k, base + 4, k, lp), lp)
                else:
                    for k in range(4):
                        unit(dn + k, y_evac(dn + k, base + 4, k))
                dve.wait_ge(evacuated, UT * (dn + 4))
                postnorm(2 * layer + 1, 4 * layer + 3, last=layer == 1)
                if layer == 0:
                    dve.wait_ge(x_ready, 8)


def kernel(**a):
    import concourse.bacc as bacc
    from concourse.bass_utils import run_bass_kernel_spmd

    a = {k: np.asarray(v) for k, v in a.items()}

    def chunks(w):
        k, n = w.shape
        return w.reshape(k // (CK * P), CK, P, n // UNIT, UNIT).transpose(3, 0, 2, 1, 4).reshape(n // UNIT, -1, P, CW)

    def by_partition(v):
        return np.ascontiguousarray(np.moveaxis(v.reshape(*v.shape[:-1], -1, P), -1, 0))

    hd, kd = NH * HD, GROUPS * HD
    win0, win1 = a["swa_w_in"][0], a["nsa_w_in"][0]
    parts = []
    for layer in range(2):
        if layer == 0:
            parts += [chunks(win0[:, hd:]), chunks(win0[:, :hd]), chunks(a["swa_w_o"][0])]
        else:
            parts += [chunks(win1[:, hd:hd + 6 * kd])] + [chunks(a["nsa_cmp_w1"][0, i]) for i in range(2)]
            parts += [chunks(win1[:, :hd]), chunks(a["nsa_w_o"][0])]
        gate_up = np.stack([chunks(a["ffn_w_gate"][layer]), chunks(a["ffn_w_up"][layer])], axis=1)
        parts += [gate_up, chunks(a["ffn_w_down"][layer])]
    stream = np.concatenate([p.reshape(-1, P, CW) for p in parts])
    conv = np.concatenate([a["ffn_conv_w"], a["ffn_conv_b"][:, None]], axis=1)
    conv = conv.reshape(2, 4, NF, UT, P).transpose(4, 0, 2, 3, 1).reshape(P, 2, NF, UT * 4)
    arrays = {
        "x": by_partition(a["x"][0]).transpose(0, 2, 1),
        "gains": by_partition(a["norm_g"].reshape(8, D)),
        "stream": stream,
        "b_in": by_partition(a["swa_b_in"][0]),
        "b_o": by_partition(a["swa_b_o"][0]),
        "sinks": a["swa_sinks"][0],
        "conv": conv,
        "pe": a["nsa_cmp_pe"][0].transpose(2, 0, 1),
        "b1": by_partition(a["nsa_cmp_b1"][0]),
        "w2": a["nsa_cmp_w2"][0].reshape(2, UT, P, HD).transpose(2, 0, 1, 3),
        "b2k": a["nsa_cmp_b2"][0, 0][:, None],
        "b2v": a["nsa_cmp_b2"][0, 1][None, :],
        "w_gates": win1[:, hd + 6 * kd:].reshape(KT, P, 96).transpose(1, 0, 2),
    }
    nc = bacc.Bacc("TRN2", target_bir_lowering=False, num_devices=1)
    args = {}
    for name, v in arrays.items():
        arrays[name] = v = np.ascontiguousarray(v)
        args[name] = nc.dram_tensor(f"in_{name}", v.shape, mybir.dt.from_np(v.dtype), kind="ExternalInput").ap()
    out = nc.dram_tensor("out_y", [P, KT, S], F32, kind="ExternalOutput").ap()
    build_program(nc, out=out, **args)
    r = run_bass_kernel_spmd(nc, [{f"in_{k}": v for k, v in arrays.items()}], core_ids=[0])
    got = r.results[0]["out_y"]
    return got.transpose(2, 1, 0).reshape(1, S, D)
```

```python
from contextlib import ExitStack

import numpy as np

import concourse.bass as bass
from concourse import mybir

F32 = mybir.dt.float32
F32R = mybir.dt.float32r
ALU = mybir.AluOpType
ACT = mybir.ActivationFunctionType

P = 128
S = 256
D = 2048
F = 5632
HD = 64
NH = 32
GROUPS = 4
HPG = NH // GROUPS
KT = D // P
FT = F // P
UNIT = 512
UT = UNIT // P
NF = F // UNIT
CK = 2
CW = CK * UNIT
RING = 4
CH = KT // CK
CHF = FT // CK
WINDOW = 128
CMP_LEN, CMP_STRIDE = 32, 16
NC = (S - CMP_LEN) // CMP_STRIDE + 1
EPS = 1e-6
FAR = 1e30
NO_KEY = 1e20
CAUSAL = S // 2 * 3
TT = S // P

KV0, Q0, O0, FF0, DN0 = 0, 1, 5, 9, 31
KC1, KS1, KW1, WK1, WV1, Q1, O1, FF1, DN1 = 35, 36, 37, 38, 39, 40, 44, 48, 70
UNITS = 74

LAG = 3


def first_chunk(u):
    longer = min(max(u - DN0, 0), 4) + min(max(u - DN1, 0), 4)
    return CH * u + (CHF - CH) * longer


CHUNKS = first_chunk(UNITS)


def attention_items(layer):
    if layer == 0:
        return [(i, "swa") for i in range(HPG)]
    return [(i, k) for i in range(HPG) for k in ("sel", "win", "cmp")]


def attention_slots(layer, last):
    steps = len(attention_items(layer)) + LAG + 2
    lo, hi = (0, 23) if last else (1, 30)
    at = [[] for _ in range(CH * UT)]
    for s in range(steps):
        at[lo + s * (hi - lo) // (steps - 1)].append(s)
    return at


def build_program(nc, x, gains, stream, b_in, b_o, sinks, conv, pe, b1, w2, b2k, b2v, w_gates, out):
    with ExitStack() as ctx:
        def sb(name, shape, dt=F32, c=ctx):
            return c.enter_context(nc.sbuf_tensor(name, [P] + shape if isinstance(shape, list) else shape, dt))

        def sem(name):
            return ctx.enter_context(nc.semaphore(name))

        sets = [ctx.enter_context(nc.psum_tensor(f"set{i}", [P, UT, 512], F32)) for i in range(2)]
        ps_scores = [sets[1][:, 0, :], sets[1][:, 1, :]]
        ps_turned = sets[1][:, 2, :]
        ps_o = sets[1][:, 3, :]
        ps_mean = sets[0][:, 0, 0:S]
        ps_mean_x = [sets[1][:, 1, 0:S] if n % 2 else sets[0][:, 1, 0:S] for n in range(4)]

        raw = sb("raw", [RING, CW])
        whi = sb("whi", [RING, CW], F32R)
        wlo = sb("wlo", [RING, CW], F32R)
        xT = sb("xT", [KT, S])
        half = sb("half", [2, UT, S])
        ones = sb("ones", [P])
        ident = sb("ident", [P])
        root = sb("root", [S])
        rnorm = sb("rnorm", [S])
        g_sb = sb("g_sb", [8, KT])
        conv_sb = sb("conv_sb", [2, NF, 4 * UT])
        b_in_sb = sb("b_in_sb", [20])
        b_q = sb("b_q", [16])
        b_o_sb = sb("b_o_sb", [KT])
        sinks_sb = sb("sinks_sb", [NH])
        neg_sinks = sb("neg_sinks", [NH])
        b1_sb = sb("b1_sb", [2, UT])
        b2k_sb = sb("b2k_sb", [1])
        b2v_sb = sb("b2v_sb", [HD])
        pe_sb = sb("pe_sb", [2, CMP_LEN])
        eps = sb("eps", [1])
        spare = sb("spare", [1])

        with ExitStack() as c:
            hs = sb("hs", [KT, 2 * S], F32R, c)
        with ExitStack() as c:
            sb("under_y", [KT, S], F32, c)
            y = sb("y", [KT, S], F32, c)
        hold = ctx.enter_context(nc.sbuf_tensor("hold_h", [P, KT * 2 * S], F32R))
        del hold

        with ExitStack() as c:
            hid = sb("hid", [FT, 2 * S], F32R, c)
            gate_in = sb("gate_in", [UT, S + 2], F32, c)
            gate = sb("gate", [UT, S], F32, c)
            cw = sb("cw", [UT, 4], F32, c)
        with ExitStack() as c:
            sb("under_squares", [FT, 2 * S], F32, c)
            squares = sb("squares", [UT, S], F32, c)
            sq_sum = sb("sq_sum", [UT, S], F32, c)
        with ExitStack() as c:
            with ExitStack() as c2:
                os_ = sb("os", [KT, 2 * S], F32R, c2)
            with ExitStack() as c2:
                wg_split = sb("wg_split", [KT, 2, 96], F32R, c2)
                blocks = [sb(f"blocks{i}", [KT, 2, GROUPS * NC], F32R, c2) for i in range(2)]
                kc_raw = sb("kc_raw", [2, 2, S], F32, c2)
            sb("hold_o", [KT * 2 * S], F32R, c)
            with ExitStack() as c2:
                qg = sb("qg", [UT, S], F32, c2)
            with ExitStack() as c2:
                block_f = sb("block_f", [KT, GROUPS * NC], F32, c2)
            sb("hold_q", [UT * S], F32, c)
            k_raw = sb("k_raw", [2, 2, S], F32, c)
            v_raw = sb("v_raw", [2, 2, S], F32, c)
            k_dup = sb("k_dup", [2, GROUPS, S], F32, c)
            v_nat = sb("v_nat", [2, TT, S], F32, c)
            k_g = sb("k_g", [2, S], F32, c)
            v_g = sb("v_g", [2, TT, HD], F32, c)
            kc_all = sb("kc_all", [GROUPS * NC], F32, c)
            vc_all = sb("vc_all", [GROUPS * HD], F32, c)
            kc_g = sb("kc_g", [NC], F32, c)
            vc_g = sb("vc_g", [HD], F32, c)
            gates = sb("gates", [TT, 96], F32, c)
            gates_g = sb("gates_g", [TT, 24], F32, c)
            sinks_g = sb("sinks_g", [HPG], F32, c)
            neg_sinks_g = sb("neg_sinks_g", [HPG], F32, c)
            dist = sb("dist", [CAUSAL], F32, c)
            bias = sb("bias", [HPG, CAUSAL], F32, c)
            bias_c = sb("bias_c", [HPG, 2 * NC], F32, c)
            with ExitStack() as c2:
                scored = sb("scored", [2, CAUSAL], F32, c2)
                probs = sb("probs", [LAG, CAUSAL], F32, c2)
                turned = sb("turned", [2, CAUSAL], F32, c2)
            with ExitStack() as c2:
                wg_raw = sb("wg_raw", [KT, 96], F32, c2)
            sb("hold_s", [(4 + LAG) * CAUSAL], F32, c)
            neg_max = sb("neg_max", [2, TT], F32, c)
            sums = sb("sums", [2, TT], F32, c)
            sink_e = sb("sink_e", [2, TT], F32, c)
            total = sb("total", [2, TT], F32, c)
            recip = sb("recip", [2, TT], F32, c)
            neg_r = sb("neg_r", [TT], F32, c)
            cmp_z = sb("cmp_z", [UT, GROUPS * NC], F32, c)
            cmp_h = sb("cmp_h", [2, UT, GROUPS * NC], F32, c)
            w2k_sb = sb("w2k_sb", [UT, P], F32, c)
            w2v_sb = sb("w2v_sb", [UT, HD], F32, c)

        raw_in = [sem(f"raw_in{i}") for i in range(RING)]
        hi_ready, lo_ready, chunk_used = sem("hi_ready"), sem("lo_ready"), sem("chunk_used")
        half_ready, evacuated = sem("half_ready"), sem("evacuated")
        const_in, late_in, filled = sem("const_in"), sem("late_in"), sem("filled")
        x_in = [sem(f"x_in{q}") for q in range(4)]
        prepared = sem("prepared")
        x_ready, sq_ready, sq_used, mean_ready = sem("x_ready"), sem("sq_ready"), sem("sq_used"), sem("mean_ready")
        root_ready, rnorm_ready = sem("root_ready"), sem("rnorm_ready")
        hf_ready, h_hi_ready, h_ready = sem("hf_ready"), sem("h_hi_ready"), sem("h_ready")
        y_sq_ready, sq_sum_ready, y_scaled = sem("y_sq_ready"), sem("sq_sum_ready"), sem("y_scaled")
        k_dup_ready, v_turned, v_ready = sem("k_dup_ready"), sem("v_turned"), sem("v_ready")
        staged, bias_ready = sem("staged"), sem("bias_ready")
        scores_ready, scores_read, exp_ready = sem("scores_ready"), sem("scores_read"), sem("exp_ready")
        total_ready, recip_ready, probs_ready = sem("total_ready"), sem("recip_ready"), sem("probs_ready")
        probs_turned, turned_copied = sem("probs_turned"), sem("turned_copied")
        o_ready, o_hi_ready, o_read = sem("o_ready"), sem("o_hi_ready"), sem("o_read")
        cw_ready, conv_step, gate_ready = sem("cw_ready"), sem("conv_step"), sem("gate_ready")
        hid_f, hid_hi, hid_ready = sem("hid_f"), sem("hid_hi"), sem("hid_ready")
        block_built, block_hi, block_ready = sem("block_built"), sem("block_hi"), sem("block_ready")
        cmp_h_ready, cleared = sem("cmp_h_ready"), sem("cleared")
        wg_hi, wg_ready, kc_done, gate_dot, kc_ready = sem("wg_hi"), sem("wg_ready"), sem("kc_done"), sem("gate_dot"), sem("kc_ready")
        vc_ready, gate_exp, gate_plus, gates_ready = sem("vc_ready"), sem("gate_exp"), sem("gate_plus"), sem("gates_ready")
        rnorm_turned, neg_r_ready, q_summed = sem("rnorm_turned"), sem("neg_r_ready"), sem("q_summed")
        summed, ffn_scaled = sem("summed"), sem("ffn_scaled")
        passed_dve, passed_pool = sem("passed_dve"), sem("passed_pool")
        out_ready, out_done = sem("out_ready"), sem("out_done")

        N_CONST = 11

        def items_before(layer, g=0):
            return (0 if layer == 0 else GROUPS * HPG) + g * len(attention_items(layer))

        def bias_before(layer):
            return 0 if layer == 0 else HPG + 3 * HPG

        n_bias = [HPG, 2 * HPG]
        n_staged = [4, 7]

        def staged_after(layer, g):
            return (0 if layer == 0 else GROUPS * n_staged[0]) + n_staged[layer] * (g + 1)

        def set_of(u):
            if u in (KV0, KC1, KW1, WV1):
                return 1
            if Q0 <= u <= O0 or Q1 <= u <= O1 or u in (KS1, WK1):
                return 0
            base = next(b for b in (DN1, FF1, O1, DN0, FF0, O0) if u >= b)
            return (u - base) % 2

        def before_in_set(u):
            for v in range(u - 1, -1, -1):
                if set_of(v) == set_of(u):
                    return v
            return None

        block = ctx.enter_context(nc.Block())

        @block.sync
        def _(sp):
            for q in range(4):
                sp.dma_start(xT[:, q * 4:(q + 1) * 4, :], x[:, q * 4:(q + 1) * 4, :]).then_inc(x_in[q], 16)
            for s in range(RING):
                sp.dma_start(raw[:, s, :], stream[s]).then_inc(raw_in[s], 16)
            turns = stream.rearrange("(n s) p c -> n s p c", s=RING)
            with sp.Fori(0, CHUNKS // RING - 1) as n:
                for s in range(RING):
                    sp.wait_ge(lo_ready, n * RING + (s + 1))
                    sp.dma_start(raw[:, s, :], turns[n + 1, s]).then_inc(raw_in[s], 16)
            for q in range(4):
                sp.wait_ge(out_ready, q + 1)
                sp.dma_start(out[:, q * 4:(q + 1) * 4, :], xT[:, q * 4:(q + 1) * 4, :]).then_inc(out_done, 16)
            sp.wait_ge(out_done, 64)

        @block.gpsimd
        def _(pool):
            nc.gpsimd.memset(ones[:], 1.0).then_inc(filled, 1)
            nc.gpsimd.memset(eps[:], EPS).then_inc(filled, 1)
            nc.gpsimd.memset(ident[:], 0.0).then_inc(filled, 1)
            pool.wait_ge(filled, 3)
            nc.gpsimd.affine_select(out=ident[:], in_=ident[:], compare_op=ALU.not_equal, fill=1.0, base=0,
                                    pattern=[[-1, P]], channel_multiplier=1).then_inc(filled, 1)
            pool_sem = [0]
            made = sem("made")

            def step(ins):
                pool_sem[0] += 1
                ins.then_inc(made, 1)
                pool.wait_ge(made, pool_sem[0])

            def causal(t, window):
                step(nc.gpsimd.affine_select(out=t[:, 0:P], in_=t[:, 0:P], compare_op=ALU.is_ge, fill=FAR,
                                             base=0, pattern=[[-1, P]], channel_multiplier=1))
                last = nc.gpsimd.affine_select(out=t[:, P:], in_=t[:, P:], compare_op=ALU.is_ge, fill=FAR,
                                               base=P, pattern=[[-1, S]], channel_multiplier=1)
                if window:
                    step(last)
                    last = nc.gpsimd.affine_select(out=t[:, P:], in_=t[:, P:], compare_op=ALU.is_ge, fill=FAR,
                                                   base=WINDOW - 1 - P, pattern=[[1, S]], channel_multiplier=-1)
                return last

            def bias_tables(layer):
                step(nc.gpsimd.iota(dist[:, 0:P], pattern=[[-1, P]], base=0, channel_multiplier=1,
                                    allow_small_or_imprecise_dtypes=True))
                step(nc.gpsimd.iota(dist[:, P:], pattern=[[-1, S]], base=P, channel_multiplier=1,
                                    allow_small_or_imprecise_dtypes=True))
                for i in range(HPG):
                    slope = float(np.exp2(np.float32(-8.0 * (i + 1) / NH)))
                    step(nc.gpsimd.tensor_scalar(bias[:, i, :], dist[:], slope, 1.0, ALU.mult, ALU.mult))
                    causal(bias[:, i, :], layer == 0).then_inc(bias_ready, 1)
                if layer == 1:
                    step(nc.gpsimd.iota(dist[:, 0:2 * NC].rearrange("p (t n) -> p t n", t=TT),
                                        pattern=[[P, TT], [-CMP_STRIDE, NC]], base=1 - CMP_LEN, channel_multiplier=1,
                                        allow_small_or_imprecise_dtypes=True))
                    for i in range(HPG):
                        slope = float(np.exp2(np.float32(-8.0 * (i + 1) / NH)))
                        step(nc.gpsimd.tensor_scalar(bias_c[:, i, :], dist[:, 0:2 * NC], slope, 1.0, ALU.mult, ALU.mult))
                        t = bias_c[:, i, :].rearrange("p (t n) -> p t n", t=TT)
                        nc.gpsimd.affine_select(out=t, in_=t, compare_op=ALU.is_ge, fill=FAR, base=1 - CMP_LEN,
                                                pattern=[[P, TT], [-CMP_STRIDE, NC]],
                                                channel_multiplier=1).then_inc(bias_ready, 1)

            def stage(layer, g):
                pool.wait_ge(o_ready, items_before(layer, g))
                cp = nc.gpsimd.tensor_copy
                cp(k_g[:, 0, :], k_dup[:, 0, g, :]).then_inc(staged, 1)
                cp(v_g[:, 0, :, :], v_nat[:, 0, :, bass.ds(g * HD, HD)]).then_inc(staged, 1)
                if layer == 0:
                    cp(sinks_g[:], sinks_sb[:, bass.ds(g * HPG, HPG)]).then_inc(staged, 1)
                    cp(neg_sinks_g[:], neg_sinks[:, bass.ds(g * HPG, HPG)]).then_inc(staged, 1)
                    return
                cp(k_g[:, 1, :], k_dup[:, 1, g, :]).then_inc(staged, 1)
                cp(v_g[:, 1, :, :], v_nat[:, 1, :, bass.ds(g * HD, HD)]).then_inc(staged, 1)
                cp(kc_g[:], kc_all[:, bass.ds(g * NC, NC)]).then_inc(staged, 1)
                cp(vc_g[0:NC, :], vc_all[0:NC, bass.ds(g * HD, HD)]).then_inc(staged, 1)
                cp(gates_g[:], gates[:, :, bass.ds(g * 24, 24)]).then_inc(staged, 1)

            for layer in range(2):
                if layer == 1:
                    pool.wait_ge(chunk_used, first_chunk(KC1))
                bias_tables(layer)
                pool.wait_ge(k_dup_ready, 1 if layer == 0 else 3)
                pool.wait_ge(v_ready, 1 if layer == 0 else 3)
                if layer == 0:
                    pool.wait_ge(prepared, 1)
                else:
                    pool.wait_ge(kc_ready, 1)
                    pool.wait_ge(vc_ready, 1)
                    pool.wait_ge(gates_ready, 1)
                stage(layer, 0)
                items = attention_items(layer)
                with pool.Fori(0, GROUPS - 1) as g:
                    for n, (i, kind) in enumerate(items):
                        if kind == "sel":
                            continue
                        pool.wait_ge(scores_read, g * len(items) + (items_before(layer) + n + 1))
                        pool.sem_inc(passed_pool, 1)
                        t = bias_c[:, i, :] if kind == "cmp" else bias[:, i, :]
                        nc.gpsimd.tensor_scalar(t, t, 0.25, 1.0, ALU.mult, ALU.mult).then_inc(bias_ready, 1)
                    stage(layer, g + 1)
                ff = FF0 if layer == 0 else FF1
                pool.wait_ge(chunk_used, first_chunk(ff))
                nc.gpsimd.tensor_copy(cw[:].rearrange("p a b -> p (a b)"), conv_sb[:, layer, 0, :]).then_inc(cw_ready, 1)
                with pool.Fori(1, NF) as f:
                    pool.wait_ge(conv_step, f * 3 + layer * 3 * NF)
                    nc.gpsimd.tensor_copy(cw[:].rearrange("p a b -> p (a b)"),
                                          conv_sb[:, layer, f, :]).then_inc(cw_ready, 1)

        @block.tensor
        def _(pe):
            mm = nc.tensor.matmul

            def chunk(c, last_c, g, slot, u, rhs, width, kt0, at, tile_before=None):
                w = width
                for t in range(UT):
                    if tile_before:
                        tile_before(c * UT + t)
                    if c == 0 and at is not None:
                        pe.wait_ge(evacuated, at + t)
                    if t == 0:
                        pe.wait_ge(lo_ready, g + 1)
                    bank = sets[set_of(u)][:, t, :]
                    for j in range(CK):
                        cols = slice(j * UNIT + t * P, j * UNIT + (t + 1) * P)
                        first, final = c == 0 and j == 0, c == last_c and j == CK - 1
                        r = rhs(kt0 + j)

                        def high():
                            return mm(bank[:, 0:2 * w], whi[:, slot, cols], r, start=first, stop=final)

                        def low():
                            return mm(bank[:, w:2 * w], wlo[:, slot, cols], r[:, 0:w], start=False, stop=False)

                        if final:
                            low()
                            last = high()
                        else:
                            high()
                            last = low()
                last.then_inc(chunk_used, 1)

            def unit(u, source, lp=None, width=S, waits=None, tile_before=None, after_chunk=None):
                n = CHF if source is hid else CH
                v = before_in_set(u)
                more_g, more_e = (lp[0] * lp[1], lp[0] * lp[2]) if lp else (0, 0)
                at = None if v is None else more_e + (UT * v + 1)
                for c in range(n):
                    g0 = first_chunk(u) + c
                    if waits:
                        waits(c)
                    chunk(c, n - 1, more_g + g0, g0 % RING, u, lambda kt: source[:, kt, :], width, CK * c, at,
                          tile_before)
                    if after_chunk:
                        after_chunk(c)

            def sum_squares(out, tile, first, last):
                for t in range(UT):
                    ins = mm(out, ones[:], tile[:, t, :], start=first and t == 0, stop=last and t == UT - 1)
                return ins

            def x_squares(n, q):
                pe.wait_ge(sq_ready, 4 * n + q + 1)
                ins = sum_squares(ps_mean_x[n], sq_sum if q % 2 else squares, q == 0, q == 3)
                ins.then_inc(sq_used if q < 3 else mean_ready, 1)

            def x_squares_after(n):
                return lambda c: x_squares(n, (1, 3, 5, 6).index(c)) if c in (1, 3, 5, 6) else None

            def postnorm(n):
                pe.wait_ge(sq_sum_ready, 4 * n + 4)
                sum_squares(ps_mean, sq_sum, True, True).then_inc(mean_ready, 1)

            def h_waits(n):
                return lambda c: pe.wait_ge(h_ready, 4 * n + (CK * c) // 4 + 1)

            def attention(layer, u_q, g, last):
                items = attention_items(layer)
                ib = items_before(layer) + g * len(items)
                pairs = 16 * layer + 4 * g
                at = attention_slots(layer, last)

                def scores(s):
                    i, kind = items[s]
                    hp = slice((i % 2) * HD, (i % 2) * HD + HD)
                    if s == 0:
                        pe.wait_ge(evacuated, u_q)
                        pe.wait_ge(staged, staged_after(layer, g))
                    if s >= 2:
                        pe.wait_ge(scores_read, ib + (s - 1))
                    q = qg[hp, i // 2, :]
                    b = ps_scores[s % 2]
                    if kind == "cmp":
                        mm(b[:, 0:NC], q[:, 0:P], kc_g[hp, :], start=True, stop=True)
                        ins = mm(b[:, NC:2 * NC], q[:, P:S], kc_g[hp, :], start=True, stop=True)
                    else:
                        k = k_g[hp, 1 if kind == "win" else 0, :]
                        mm(b[:, 0:P], q[:, 0:P], k[:, 0:P], start=True, stop=True)
                        ins = mm(b[:, P:CAUSAL], q[:, P:S], k, start=True, stop=True)
                    ins.then_inc(scores_ready, 1)

                def turn(s):
                    kind = items[s][1]
                    pe.wait_ge(probs_ready, ib + (s + 1))
                    if s >= 1:
                        pe.wait_ge(turned_copied, ib + s)
                    e = probs[:, s % LAG, :]
                    if kind == "cmp":
                        for t in range(TT):
                            ins = nc.tensor.transpose(ps_turned[0:NC, t * P:(t + 1) * P], e[:, t * NC:(t + 1) * NC],
                                                      ident[:])
                    else:
                        for t in range(3):
                            ins = nc.tensor.transpose(ps_turned[:, t * P:(t + 1) * P], e[:, t * P:(t + 1) * P], ident[:])
                    ins.then_inc(probs_turned, 1)

                def outputs(s):
                    i, kind = items[s]
                    hp = slice((i % 2) * HD, (i % 2) * HD + HD)
                    first = kind in ("swa", "sel")
                    pe.wait_ge(turned_copied, ib + (s + 1))
                    if first and i % 2 == 0:
                        pe.wait_ge(o_read, 1 + pairs + i // 2)
                    e = turned[:, s % 2, :]
                    if kind == "cmp":
                        ins = mm(ps_o[hp, 0:S], vc_g[0:NC, :], e[0:NC, 0:S], start=False, stop=True)
                    else:
                        v = v_g[:, 1 if kind == "win" else 0]
                        mm(ps_o[hp, 0:S], v[:, 0, :], e[:, 0:S], start=first, stop=False)
                        ins = mm(ps_o[hp, P:S], v[:, 1, :], e[:, S:CAUSAL], start=False, stop=kind == "swa")
                    ins.then_inc(o_ready, 1)

                def before(tile):
                    for s in at[tile]:
                        if LAG <= s < len(items) + LAG:
                            turn(s - LAG)
                        if s < len(items):
                            scores(s)
                        if LAG + 1 <= s < len(items) + LAG + 1:
                            outputs(s - LAG - 1)

                return before

            def turn_values(which, b):
                for tt in range(TT):
                    for f in range(2):
                        ins = nc.tensor.transpose(sets[1][:, b, tt * S + f * P:tt * S + (f + 1) * P],
                                                  v_raw[:, which, f, tt * P:(tt + 1) * P], ident[:])
                ins.then_inc(v_turned, 1)

            def after_q0(layer):
                def after(c):
                    if c != 5:
                        return
                    if layer == 0:
                        pe.wait_ge(evacuated, UT * (KV0 + 1))
                        turn_values(0, 0)
                        return
                    pe.wait_ge(evacuated, UT * (WV1 + 1))
                    turn_values(0, 0)
                    turn_values(1, 1)
                    pe.wait_ge(cmp_h_ready, 2)
                    pe.wait_ge(late_in, 16 * 4)
                    for t in range(UT):
                        ins = mm(ps_turned[:, 0:GROUPS * NC], w2k_sb[:, t, :], cmp_h[:, 0, t, :],
                                 start=t == 0, stop=t == UT - 1)
                    ins.then_inc(kc_done, 1)
                    for g in range(GROUPS):
                        o = ps_o[0:NC, g * HD:(g + 1) * HD]
                        for t in range(UT):
                            mm(o, cmp_h[:, 1, t, g * NC:(g + 1) * NC], w2v_sb[:, t, :], start=t == 0, stop=False)
                        ins = mm(o, ones[0:1, 0:NC], b2v_sb[0:1, :], start=False, stop=True)
                    pe.wait_ge(wg_ready, 1)
                    for tt in range(TT):
                        ins = nc.tensor.transpose(ps_turned[:, S + tt * P:S + (tt + 1) * P],
                                                  rnorm[:, tt * P:(tt + 1) * P], ident[:])
                    ins.then_inc(rnorm_turned, 1)
                    for tt in range(TT):
                        o = ps_o[:, S + tt * 96:S + (tt + 1) * 96]
                        for kt in range(KT):
                            hi = hs[:, kt, tt * P:(tt + 1) * P]
                            lo = hs[:, kt, S + tt * P:S + (tt + 1) * P]
                            mm(o, lo, wg_split[:, kt, 0, :], start=kt == 0, stop=False)
                            mm(o, hi, wg_split[:, kt, 1, :], start=False, stop=False)
                            ins = mm(o, hi, wg_split[:, kt, 0, :], start=False, stop=kt == KT - 1)
                    ins.then_inc(gate_dot, 1)
                return after

            for layer in range(2):
                q0, o0, ff, dn = ((Q0, O0, FF0, DN0), (Q1, O1, FF1, DN1))[layer]
                hw = h_waits(2 * layer)
                if layer == 0:
                    pe.wait_ge(filled, 4)
                    for q in range(4):
                        x_squares(0, q)
                    unit(KV0, hs, waits=hw)
                else:
                    unit(KC1, hs, waits=hw, after_chunk=x_squares_after(2))
                    pe.wait_ge(root_ready, 5)
                    unit(KS1, hs)
                    unit(KW1, hs)
                    for n, u in enumerate((WK1, WV1)):
                        pe.wait_ge(block_ready, n + 1)
                        unit(u, blocks[n][:].rearrange("p k a b -> p k (a b)"), width=GROUPS * NC)
                unit(q0, hs, after_chunk=after_q0(layer))
                if layer == 1:
                    pe.wait_ge(kc_ready, 1)
                    pe.wait_ge(vc_ready, 1)
                    pe.wait_ge(gate_exp, 1)
                pe.wait_ge(v_ready, 1 if layer == 0 else 3)
                with pe.Fori(0, GROUPS - 1) as g:
                    unit(q0 + 1, hs, lp=(g, CH, UT), tile_before=attention(layer, g * UT + UT * (q0 + 1), g, False))

                def o_waits(c):
                    if c >= 6:
                        pe.wait_ge(o_read, 1 + 16 * layer + CK * c + 2)
                    elif c == 0:
                        pe.wait_ge(o_read, 1 + 16 * layer + 12)

                g = GROUPS - 1
                unit(o0, os_, waits=o_waits, tile_before=attention(layer, UT * (q0 + g + 1), g, True))
                for u in range(o0 + 1, o0 + 4):
                    unit(u, os_)
                postnorm(2 * layer)
                unit(ff, hs, waits=h_waits(2 * layer + 1), after_chunk=x_squares_after(2 * layer + 1))
                pe.wait_ge(root_ready, 4 * layer + 3)
                unit(ff + 1, hs)
                with pe.Fori(0, NF - 1) as f:
                    for u in (ff + 2, ff + 3):
                        unit(u, hs, lp=(f, 2 * CH, 2 * UT))

                def hid_waits(c):
                    if c % 2 == 0 and c // 2 >= NF - 2:
                        pe.wait_ge(hid_ready, NF * layer + c // 2 + 1)
                    elif c == 0:
                        pe.wait_ge(hid_ready, NF * layer + NF - 2)

                if layer == 0:
                    with pe.Fori(0, 2) as i:
                        for u in (dn, dn + 1):
                            unit(u, hid, lp=(i, 2 * CHF, 2 * UT), waits=hid_waits if u == dn else None)
                else:
                    for u in range(dn, dn + 4):
                        unit(u, hid, waits=hid_waits if u == dn else None)
                postnorm(2 * layer + 1)

        @block.scalar
        def _(act):
            A = nc.scalar.activation
            consts = ((g_sb, gains), (conv_sb, conv), (b_in_sb, b_in), (b_o_sb, b_o),
                      (sinks_sb, sinks.partition_broadcast(P)), (b1_sb, b1))
            for dst, src in consts:
                act.dma_start(dst[:], src).then_inc(const_in, 16)
            for h in range(2):
                half_p = slice(h * HD, (h + 1) * HD)
                act.dma_start(pe_sb[half_p], pe).then_inc(const_in, 16)
                act.dma_start(b2k_sb[half_p, :], b2k).then_inc(const_in, 16)
            act.dma_start(b2v_sb[0:1, :], b2v).then_inc(const_in, 16)

            def split(g0, more=0, turn=0):
                slot = g0 % RING
                act.wait_ge(raw_in[slot], turn + 16 * (g0 // RING + 1))
                if g0 >= RING:
                    act.wait_ge(chunk_used, more + (g0 - RING + 1))
                A(whi[:, slot, :], raw[:, slot, :], ACT.Copy).then_inc(hi_ready, 1)

            def loop_terms(lp):
                return (lp[0] * lp[1], lp[0] * (lp[1] // RING * 16), lp[0] * lp[2]) if lp else (0, 0, 0)

            def unit_first_half(u, lp=None, bias_of=None, scale=1.0, width=S):
                more, _, more_e = loop_terms(lp)
                n = CHF if (DN0 <= u < DN0 + 4 or u >= DN1) else CH
                act.wait_ge(chunk_used, more + (first_chunk(u) + n))
                st = set_of(u)
                if bias_of is None:
                    if scale == 1.0:
                        A(half[:, st, :, 0:width], sets[st][:, :, 0:width], ACT.Copy).then_inc(half_ready, UT)
                    else:
                        for t in range(UT):
                            A(half[:, st, t, :], sets[st][:, t, 0:S], ACT.Copy, scale=scale).then_inc(half_ready, 1)
                else:
                    for t in range(UT):
                        A(half[:, st, t, :], sets[st][:, t, 0:S], ACT.Identity, bias=bias_of(t),
                          scale=scale).then_inc(half_ready, 1)

            def unit(u, evac, lp=None, done=RING):
                more, turn, _ = loop_terms(lp)
                n = CHF if (DN0 <= u < DN0 + 4 or u >= DN1) else CH
                g0 = first_chunk(u)
                last = u == UNITS - 1
                for c in range(done, n + (0 if last else RING - 1)):
                    split(g0 + c, more, turn)
                evac()
                if not last:
                    split(g0 + n + RING - 1, more, turn)

            def finish_norm(mean, k):
                A(spare[:], eps[:], ACT.Sqrt)
                act.wait_ge(mean_ready, k + 1)
                A(root[:], mean, ACT.Sqrt, bias=eps[:], scale=1.0 / D).then_inc(root_ready, 1)

            def x_squares(n, q):
                if q >= 2:
                    act.wait_ge(sq_used, 3 * n + q - 1)
                A(sq_sum[:] if q % 2 else squares[:], xT[:, q * 4:(q + 1) * 4, :], ACT.Square).then_inc(sq_ready, 1)

            def first_norm():
                for q in range(4):
                    act.wait_ge(x_in[q], 16)
                    x_squares(0, q)
                act.wait_ge(filled, 4)
                finish_norm(ps_mean_x[0], 0)
                for q in range(4):
                    act.wait_ge(hf_ready, q + 1)
                    A(hs[:, q * 4:(q + 1) * 4, 0:S], half[:, q % 2], ACT.Copy).then_inc(h_hi_ready, 1)

            def prenorm(n, gain, u):
                g0 = first_chunk(u)
                for q in range(4):
                    act.wait_ge(x_ready, 4 * (n - 1) + q + 1)
                    for t in range(UT):
                        kt = q * 4 + t
                        ins = A(hs[:, kt, 0:S], xT[:, kt, :], ACT.Copy, scale=g_sb[:, gain, kt:kt + 1])
                    ins.then_inc(h_hi_ready, 1)
                    x_squares(n, q)
                    for c in ((), (4,), (5,), (6, 7))[q]:
                        split(g0 + c)

            def y_evac(u, base, k, lp=None, bias_of=None):
                def evac():
                    unit_first_half(u, lp, bias_of)
                    st = set_of(u)
                    i, per = (lp[0], 2) if lp else (0, 0)
                    more_e = lp[0] * lp[2] if lp else 0
                    act.wait_ge(evacuated, more_e + UT * (u + 1))
                    if base + k >= 1:
                        act.wait_ge(sq_sum_ready, i * per + (base + k))
                    A(squares[:], y[:, bass.ds(i * (per * UT) + k * UT, UT), :], ACT.Square).then_inc(y_sq_ready, 1)
                return evac

            def attention(layer, g, last):
                items = attention_items(layer)
                ib = items_before(layer) + g * len(items)
                pairs = 16 * layer + 4 * g
                at = attention_slots(layer, last)

                def copy_turned(s):
                    act.wait_ge(probs_turned, ib + (s + 1))
                    if s >= 2:
                        act.wait_ge(o_ready, ib + (s - 1))
                    if items[s][1] == "cmp":
                        A(turned[0:NC, s % 2, 0:S], ps_turned[0:NC, 0:S], ACT.Copy).then_inc(turned_copied, 1)
                    else:
                        A(turned[:, s % 2, :], ps_turned[:, 0:CAUSAL], ACT.Copy).then_inc(turned_copied, 1)

                def exponents(s):
                    i, kind = items[s]
                    act.wait_ge(scores_read, ib + (s + 1))
                    b = s % 2
                    ends = (0, NC, 2 * NC) if kind == "cmp" else (0, P, CAUSAL)
                    for t in range(TT):
                        cols = slice(ends[t], ends[t + 1])
                        ins = A(probs[:, s % LAG, cols], scored[:, b, cols], ACT.Exp, bias=neg_max[:, b, t:t + 1],
                                scale=-1.0, accum_out=sums[:, b, t:t + 1])
                    if kind == "swa":
                        ins = A(sink_e[:, b, :], neg_max[:, b, :], ACT.Exp, bias=sinks_g[:, i:i + 1])
                    ins.then_inc(exp_ready, 1)

                def pair_high(s):
                    p = items[s][0] // 2
                    act.wait_ge(o_ready, ib + (s + 1))
                    A(os_[:, bass.ds(g * 4 + p, 1), 0:S].rearrange("p a b -> p (a b)"), ps_o[:, 0:S],
                      ACT.Copy).then_inc(o_hi_ready, 1)

                def step(tile):
                    for s in at[tile]:
                        if s == 0:
                            act.wait_ge(staged, staged_after(layer, g))
                        if LAG <= s < len(items) + LAG:
                            copy_turned(s - LAG)
                        o = s - LAG - 2
                        if o >= 0 and items[o][0] % 2 == 1 and items[o][1] in ("swa", "cmp"):
                            pair_high(o)
                        if s < len(items):
                            exponents(s)

                return step

            def attention_unit(u, evac, step, lp=None):
                more, turn, _ = loop_terms(lp)
                g0 = first_chunk(u)
                for tile in range(CH * UT):
                    step(tile)
                    if tile >= UT and tile % UT == 0:
                        split(g0 + RING + tile // UT - 1, more, turn)
                evac()
                split(g0 + CH + RING - 1, more, turn)

            for g in range(RING):
                split(g)
            act.wait_ge(const_in, 16 * N_CONST)
            for layer in range(2):
                q0, o0, ff, dn = ((Q0, O0, FF0, DN0), (Q1, O1, FF1, DN1))[layer]
                if layer == 0:
                    first_norm()
                    unit(KV0, lambda: unit_first_half(KV0, bias_of=lambda t: b_in_sb[:, 16 + t:17 + t]))
                else:
                    prenorm(2, 4, KC1)

                    def kc_evac():
                        finish_norm(ps_mean_x[2], 4)
                        act.dma_start(wg_raw[:], w_gates).then_inc(late_in, 16)
                        act.dma_start(w2k_sb[:, :, 0:HD], w2[:, 0]).then_inc(late_in, 16)
                        act.dma_start(w2k_sb[:, :, HD:P], w2[:, 0]).then_inc(late_in, 16)
                        act.dma_start(w2v_sb[:], w2[:, 1]).then_inc(late_in, 16)
                        unit_first_half(KC1)

                    unit(KC1, kc_evac, done=CH)
                    for n, u in enumerate((KS1, KW1)):
                        unit(u, lambda u=u: unit_first_half(u))
                        act.wait_ge(block_built, n + 1)
                        A(blocks[n][:, :, 0, :], block_f[:], ACT.Copy).then_inc(block_hi, 1)
                        if n == 0:
                            act.wait_ge(late_in, 64)
                            A(wg_split[:, :, 0, :], wg_raw[:], ACT.Copy).then_inc(wg_hi, 1)
                    for n, u in enumerate((WK1, WV1)):
                        def evac(u=u, n=n):
                            unit_first_half(u, width=GROUPS * NC)
                            act.wait_ge(evacuated, UT * (u + 1))
                            A(cmp_h[:, n], cmp_z[:], ACT.Gelu_apprx_tanh).then_inc(cmp_h_ready, 1)
                        unit(u, evac)

                def after_values():
                    if layer == 0:
                        act.wait_ge(v_turned, 1)
                        A(v_nat[:, 0].rearrange("p a b -> p (a b)"), sets[1][:, 0, :], ACT.Copy).then_inc(v_ready, 1)
                        return
                    for w in range(2):
                        act.wait_ge(v_turned, 2 + w)
                        A(v_nat[:, w].rearrange("p a b -> p (a b)"), sets[1][:, w, :], ACT.Copy).then_inc(v_ready, 1)
                    act.wait_ge(kc_done, 1)
                    A(kc_all[:], ps_turned[:, 0:GROUPS * NC], ACT.Identity, bias=b2k_sb[:]).then_inc(kc_ready, 1)
                    act.wait_ge(gate_dot, 1)
                    A(vc_all[0:NC, :], ps_o[0:NC, 0:S], ACT.Copy).then_inc(vc_ready, 1)
                    act.wait_ge(neg_r_ready, 1)
                    for tt in range(TT):
                        ins = A(gates[:, tt, :], ps_o[:, S + tt * 96:S + (tt + 1) * 96], ACT.Exp,
                                scale=neg_r[:, tt:tt + 1])
                    ins.then_inc(gate_exp, 1)

                def q_evac(u, lp=None):
                    if layer == 1:
                        return lambda: unit_first_half(u, lp)
                    if lp is None:
                        return lambda: unit_first_half(u, lp, scale=-HD ** -0.5, bias_of=lambda t: b_q[:, t:t + 1])
                    return lambda: unit_first_half(
                        u, lp, scale=-HD ** -0.5, bias_of=lambda t: b_q[:, bass.ds(lp[0] * UT + (UT + t), 1)])

                if layer == 0:
                    act.wait_ge(prepared, 1)

                def q0_evac():
                    after_values()
                    q_evac(q0)()

                unit(q0, q0_evac)
                with act.Fori(0, GROUPS - 1) as g:
                    lp = (g, CH, UT)
                    attention_unit(q0 + 1, q_evac(q0 + 1, lp), attention(layer, g, False), lp)
                bias_of = (lambda k: lambda t: b_o_sb[:, k * UT + t:k * UT + t + 1]) if layer == 0 else lambda k: None
                base = 8 * layer
                attention_unit(o0, y_evac(o0, base, 0, None, bias_of(0)), attention(layer, GROUPS - 1, True))
                for k in range(1, 4):
                    unit(o0 + k, y_evac(o0 + k, base, k, None, bias_of(k)))
                finish_norm(ps_mean, 4 * layer + 1)
                prenorm(2 * layer + 1, 4 * layer + 2, ff)

                def ffn_pair(ff, lp, f, first=False):
                    more, turn, _ = loop_terms(lp)

                    def evac():
                        if first:
                            finish_norm(ps_mean_x[2 * layer + 1], 4 * layer + 2)
                        unit_first_half(ff, lp)

                    unit(ff, evac, lp, done=CH if first else RING)
                    g0 = first_chunk(ff + 1)
                    for c in range(RING, CH):
                        split(g0 + c, more, turn)
                    act.wait_ge(conv_step, f * 3 + (3 * NF * layer + 3))
                    A(gate[:], gate[:], ACT.Silu).then_inc(gate_ready, 1)
                    for c in range(CH, CH + RING - 1):
                        split(g0 + c, more, turn)
                    unit_first_half(ff + 1, lp)
                    split(g0 + CH + RING - 1, more, turn)
                    act.wait_ge(hid_f, f + (NF * layer + 1))
                    A(hid[:, bass.ds(f * UT, UT), 0:S], gate[:], ACT.Copy).then_inc(hid_hi, 1)

                ffn_pair(ff, None, 0, True)
                with act.Fori(0, NF - 1) as f:
                    ffn_pair(ff + 2, (f, 2 * CH, 2 * UT), f + 1)
                if layer == 0:
                    with act.Fori(0, 2) as i:
                        lp = (i, 2 * CHF, 2 * UT)
                        for k in range(2):
                            unit(dn + k, y_evac(dn + k, base + 4, k, lp), lp)
                else:
                    for k in range(4):
                        unit(dn + k, y_evac(dn + k, base + 4, k))
                finish_norm(ps_mean, 4 * layer + 3)

        @block.vector
        def _(dve):
            V = nc.vector
            dve.wait_ge(const_in, 16 * N_CONST)
            V.tensor_scalar(b_q[:], b_in_sb[:, 0:16], -HD ** -0.5, None, ALU.mult).then_inc(o_read, 1)
            V.tensor_scalar(neg_sinks[:], sinks_sb[:], -1.0, None, ALU.mult).then_inc(prepared, 1)

            def split(g0, more=0):
                slot = g0 % RING
                dve.wait_ge(hi_ready, more + (g0 + 1))
                V.tensor_tensor(wlo[:, slot, :], raw[:, slot, :], whi[:, slot, :].bitcast(F32),
                                ALU.subtract).then_inc(lo_ready, 1)

            def loop_terms(lp):
                return (lp[0] * lp[1], lp[0] * lp[2]) if lp else (0, 0)

            def unit(u, evac, lp=None, done=RING):
                more, _ = loop_terms(lp)
                n = CHF if (DN0 <= u < DN0 + 4 or u >= DN1) else CH
                g0 = first_chunk(u)
                last = u == UNITS - 1
                for c in range(done, n + (0 if last else RING - 1)):
                    split(g0 + c, more)
                evac()
                if not last:
                    split(g0 + n + RING - 1, more)

            def add_halves(u, dst, lp=None, scale=None, width=S):
                _, more_e = loop_terms(lp)
                st = set_of(u)
                for t in range(UT):
                    dve.wait_ge(half_ready, more_e + (UT * u + t + 1))
                    b, h = sets[st][:, t, width:2 * width], half[:, st, t, 0:width]
                    if scale is None:
                        ins = V.tensor_tensor(dst(t), h, b, ALU.add)
                    else:
                        ins = V.scalar_tensor_tensor(dst(t), b, scale, h, ALU.mult, ALU.add)
                    ins.then_inc(evacuated, 1)

            def finish_norm(k):
                dve.wait_ge(root_ready, k + 1)
                V.reciprocal(rnorm[:], root[:]).then_inc(rnorm_ready, 1)
                dve.wait_ge(rnorm_ready, k + 1)

            def first_norm():
                n, gain = 0, 0
                finish_norm(0)

                def scaled(q):
                    for t in range(UT):
                        ins = V.scalar_tensor_tensor(half[:, q % 2, t, :], xT[:, q * 4 + t, :],
                                                     g_sb[:, gain, q * 4 + t:q * 4 + t + 1], rnorm[:], ALU.mult, ALU.mult)
                    ins.then_inc(hf_ready, 1)

                def low(q):
                    dve.wait_ge(h_hi_ready, 4 * n + q + 1)
                    V.tensor_tensor(hs[:, q * 4:(q + 1) * 4, S:2 * S], half[:, q % 2],
                                    hs[:, q * 4:(q + 1) * 4, 0:S].bitcast(F32), ALU.subtract).then_inc(h_ready, 1)

                scaled(0)
                scaled(1)
                for q in range(4):
                    low(q)
                    if q + 2 < 4:
                        dve.wait_ge(h_ready, 4 * n + q + 1)
                        scaled(q + 2)

            def row_of_r(tiles):
                return rnorm[:].unsqueeze(1).to_broadcast([P, tiles, S])

            def low_of_h(n, gain, q):
                dve.wait_ge(h_hi_ready, 4 * n + q + 1)
                for t in range(UT):
                    kt = q * 4 + t
                    ins = V.scalar_tensor_tensor(hs[:, kt, S:2 * S], xT[:, kt, :], g_sb[:, gain, kt:kt + 1],
                                                 hs[:, kt, 0:S].bitcast(F32), ALU.mult, ALU.subtract)
                ins.then_inc(h_ready, 1)

            def norms(n, gain, u=None):
                finish_norm(2 * n + 1)
                dve.wait_ge(y_scaled, 8 * n + 4)
                for q in range(4):
                    part = y[:, q * 4:(q + 1) * 4, :]
                    V.tensor_tensor(part, part, row_of_r(UT), ALU.mult).then_inc(y_scaled, 1)
                    dve.wait_ge(y_scaled, 8 * n + 4 + q + 1)
                    V.tensor_tensor(xT[:, q * 4:(q + 1) * 4, :], xT[:, q * 4:(q + 1) * 4, :], y[:, q * 4:(q + 1) * 4, :],
                                    ALU.add).then_inc(x_ready if u is not None else out_ready, 1)
                    if u is not None:
                        if q >= 1:
                            low_of_h(n + 1, gain + 1, q - 1)
                        for c in ((), (), (4,), (5,))[q]:
                            split(first_chunk(u) + c)
                if u is not None:
                    low_of_h(n + 1, gain + 1, 3)
                    split(first_chunk(u) + 6)
                    split(first_chunk(u) + 7)

            def times_r(u, t, k):
                dve.wait_ge(evacuated, UT * (u + 1))
                V.tensor_tensor(t, t, row_of_r(t.shape[1]), ALU.mult).then_inc(summed, 1)
                dve.wait_ge(summed, k)

            def y_evac(u, base, k, gain, lp=None):
                def evac():
                    i, per = (lp[0], 2) if lp else (0, 0)
                    add_halves(u, lambda t: y[:, bass.ds(i * (per * UT) + (k * UT + t), 1), :].rearrange("p a b -> p (a b)"), lp)
                    dve.wait_ge(y_sq_ready, i * per + (base + k + 1))
                    if lp is None and k == 0:
                        V.tensor_copy(sq_sum[:], squares[:]).then_inc(sq_sum_ready, 1)
                    else:
                        dve.wait_ge(sq_sum_ready, i * per + (base + k))
                        V.tensor_tensor(sq_sum[:], sq_sum[:], squares[:], ALU.add).then_inc(sq_sum_ready, 1)
                    for t in range(UT):
                        tile = y[:, bass.ds(i * (per * UT) + (k * UT + t), 1), :].rearrange("p a b -> p (a b)")
                        g1 = g_sb[:, gain, k * UT + t:k * UT + t + 1] if lp is None else g_sb[:, gain, bass.ds(i * (per * UT) + (k * UT + t), 1)]
                        ins = V.tensor_scalar(tile, tile, g1, None, ALU.mult)
                    ins.then_inc(y_scaled, 1)
                return evac

            def attention(layer, g, last):
                items = attention_items(layer)
                ib = items_before(layer) + g * len(items)
                at = attention_slots(layer, last)
                tb = 8 * GROUPS * layer + g * HPG

                def add_bias(s):
                    i, kind = items[s]
                    b = s % 2
                    dve.wait_ge(scores_ready, ib + (s + 1))
                    if s == 0:
                        dve.wait_ge(bias_ready, bias_before(layer) + n_bias[layer] * (g + 1))
                        dve.wait_ge(staged, staged_after(layer, g))
                    dve.sem_inc(passed_dve, 1)
                    ends = (0, NC, 2 * NC) if kind == "cmp" else (0, P, CAUSAL)
                    table = bias_c if kind == "cmp" else bias
                    for t in range(TT):
                        cols = slice(ends[t], ends[t + 1])
                        ins = V.tensor_tensor_reduce(
                            out=scored[:, b, cols], in0=ps_scores[b][:, cols], in1=table[:, i, cols], scale=1.0,
                            scalar=neg_sinks_g[:, i:i + 1] if kind == "swa" else NO_KEY,
                            op0=ALU.add, op1=ALU.min, accum_out=neg_max[:, b, t:t + 1])
                    ins.then_inc(scores_read, 1)

                def normalize(s):
                    i, kind = items[s]
                    b = s % 2
                    dve.wait_ge(exp_ready, ib + (s + 1))
                    tot = sums
                    if kind == "swa":
                        V.tensor_tensor(total[:, b, :], sums[:, b, :], sink_e[:, b, :], ALU.add).then_inc(total_ready, 1)
                    elif kind == "cmp":
                        V.tensor_scalar(total[:, b, :], sums[:, b, :], 1e-30, None, ALU.max).then_inc(total_ready, 1)
                    if kind in ("swa", "cmp"):
                        tot = total
                        dve.wait_ge(total_ready, tb + (i + 1))
                    V.reciprocal(recip[:, b, :], tot[:, b, :]).then_inc(recip_ready, 1)
                    dve.wait_ge(recip_ready, ib + (s + 1))
                    ends = (0, NC, 2 * NC) if kind == "cmp" else (0, P, CAUSAL)
                    which = {"cmp": 0, "sel": 1, "win": 2}
                    for t in range(TT):
                        e = probs[:, s % LAG, ends[t]:ends[t + 1]]
                        r = recip[:, b, t:t + 1]
                        if kind == "swa":
                            ins = V.tensor_scalar(e, e, r, None, ALU.mult)
                        else:
                            c = 3 * i + which[kind]
                            ins = V.tensor_scalar(e, e, r, gates_g[:, t, c:c + 1], ALU.mult, ALU.mult)
                    ins.then_inc(probs_ready, 1)

                def pair_low(s):
                    p = items[s][0] // 2
                    dve.wait_ge(o_hi_ready, 16 * layer + 4 * g + (p + 1))
                    at_pair = os_[:, bass.ds(g * 4 + p, 1), :].rearrange("p a b -> p (a b)")
                    V.tensor_tensor(at_pair[:, S:2 * S], ps_o[:, 0:S], at_pair[:, 0:S].bitcast(F32),
                                    ALU.subtract).then_inc(o_read, 1)

                def step(tile):
                    for s in at[tile]:
                        o = s - LAG - 2
                        if o >= 0 and items[o][0] % 2 == 1 and items[o][1] in ("swa", "cmp"):
                            pair_low(o)
                        if s < len(items):
                            add_bias(s)
                        if 1 <= s < len(items) + 1:
                            normalize(s - 1)

                return step

            def attention_unit(u, evac, step, lp=None):
                more, _ = loop_terms(lp)
                g0 = first_chunk(u)
                for tile in range(CH * UT):
                    step(tile)
                    if tile >= UT and tile % UT == 1:
                        split(g0 + RING + tile // UT - 1, more)
                evac()
                split(g0 + CH + RING - 1, more)

            def duplicate(which):
                for j in range(GROUPS):
                    src = k_raw[(j % 2) * HD:(j % 2) * HD + HD, which, j // 2, :]
                    for h in range(2):
                        ins = V.tensor_copy(k_dup[h * HD:(h + 1) * HD, which, j, :], src)
                ins.then_inc(k_dup_ready, 1)

            def build_blocks(n):
                for j in range(GROUPS):
                    hp = (j % 2) * HD
                    for par in range(2):
                        a = kc_raw[hp:hp + HD, n, j // 2, par:par + 1]
                        kv = bass.AP(tensor=a.tensor, offset=a.offset, ap=[a.ap[0], [2, KT], [CMP_STRIDE, NC]])
                        emb = pe_sb[hp:hp + HD, n, par:CMP_LEN:2].unsqueeze(2).to_broadcast([HD, KT, NC])
                        ins = V.tensor_tensor(block_f[par * HD:(par + 1) * HD, :, j * NC:(j + 1) * NC], kv, emb, ALU.add)
                ins.then_inc(block_built, 1)

            for g in range(RING):
                split(g)
            for layer in range(2):
                q0, o0, ff, dn = ((Q0, O0, FF0, DN0), (Q1, O1, FF1, DN1))[layer]
                if layer == 0:
                    for q in range(4):
                        dve.wait_ge(x_in[q], 16)
                    first_norm()
                    unit(KV0, lambda: add_halves(KV0, lambda t: (k_raw if t < 2 else v_raw)[:, 0, t % 2, :]))
                    dve.wait_ge(evacuated, UT * (KV0 + 1))
                    duplicate(0)
                else:
                    def kc_evac():
                        finish_norm(4)
                        add_halves(KC1, lambda t: kc_raw[:, t // 2, t % 2, :])

                    unit(KC1, kc_evac, done=CH)
                    times_r(KC1, kc_raw[:].rearrange("p a b s -> p (a b) s"), 1)
                    build_blocks(0)
                    for n, u in enumerate((KS1, KW1)):
                        unit(u, lambda: add_halves(u, lambda t: (k_raw if t < 2 else v_raw)[:, n, t % 2, :]))
                        times_r(u, k_raw[:, n], 2 * n + 2)
                        times_r(u, v_raw[:, n], 2 * n + 3)
                        duplicate(n)
                        dve.wait_ge(block_hi, n + 1)
                        V.tensor_tensor(blocks[n][:, :, 1, :], block_f[:], blocks[n][:, :, 0, :].bitcast(F32),
                                        ALU.subtract).then_inc(block_ready, 1)
                        if n == 0:
                            dve.wait_ge(block_ready, 1)
                            build_blocks(1)
                            dve.wait_ge(wg_hi, 1)
                            V.tensor_tensor(wg_split[:, :, 1, :], wg_raw[:], wg_split[:, :, 0, :].bitcast(F32),
                                            ALU.subtract).then_inc(wg_ready, 1)
                    for n, u in enumerate((WK1, WV1)):
                        w = GROUPS * NC

                        def evac():
                            for t in range(UT):
                                dve.wait_ge(half_ready, UT * (u + 1))
                                if n and t == 0:
                                    dve.wait_ge(cmp_h_ready, 1)
                                st = set_of(u)
                                V.scalar_tensor_tensor(cmp_z[:, t, :], sets[st][:, t, w:2 * w], b1_sb[:, n, t:t + 1],
                                                       half[:, st, t, 0:w], ALU.add, ALU.add).then_inc(evacuated, 1)
                        unit(u, evac)

                def q_dst(t):
                    return qg[:, t, :]

                def q_evac(u, lp):
                    if layer == 0:
                        add_halves(u, q_dst, lp, scale=-HD ** -0.5)
                        return
                    more_e = lp[0] * lp[2] if lp else 0
                    st = set_of(u)
                    dve.wait_ge(half_ready, more_e + UT * (u + 1))
                    for t in range(UT):
                        ins = V.tensor_tensor(half[:, st, t, :], half[:, st, t, :], sets[st][:, t, S:2 * S], ALU.add)
                        ins.then_inc(q_summed, 1)
                    for t in range(UT):
                        dve.wait_ge(q_summed, more_e + (UT * (u - q0) + t + 1))
                        V.scalar_tensor_tensor(qg[:, t, :], half[:, st, t, :], -HD ** -0.5, rnorm[:],
                                               ALU.mult, ALU.mult).then_inc(evacuated, 1)

                def q0_evac():
                    if layer == 1:
                        dve.wait_ge(rnorm_turned, 1)
                        dve.wait_ge(kc_ready, 1)
                        V.tensor_scalar(neg_r[:], ps_turned[:, S:2 * S].rearrange("p (t c) -> p t c", t=TT)[:, :, 0],
                                        -1.0, None, ALU.mult).then_inc(neg_r_ready, 1)
                        dve.wait_ge(gate_exp, 1)
                        V.tensor_scalar(gates[:], gates[:], 1.0, None, ALU.add).then_inc(gate_plus, 1)
                        dve.wait_ge(gate_plus, 1)
                        V.reciprocal(gates[:], gates[:]).then_inc(gates_ready, 1)
                    q_evac(q0, None)

                unit(q0, q0_evac)
                with dve.Fori(0, GROUPS - 1) as g:
                    lp = (g, CH, UT)
                    attention_unit(q0 + 1, lambda: q_evac(q0 + 1, lp),
                                   attention(layer, g, False), lp)
                base = 8 * layer
                attention_unit(o0, y_evac(o0, base, 0, 4 * layer + 1), attention(layer, GROUPS - 1, True))
                for k in range(1, 4):
                    unit(o0 + k, y_evac(o0 + k, base, k, 4 * layer + 1))
                dve.wait_ge(evacuated, UT * (o0 + 4))
                norms(2 * layer, 4 * layer + 1, ff)

                def ffn_pair(ff, lp, f, first=False):
                    more, more_e = loop_terms(lp)
                    steps = f * 3 + 3 * NF * layer
                    scaled = f * 2 + 2 * NF * layer

                    def evac():
                        if first:
                            finish_norm(4 * layer + 2)
                            V.memset(gate_in[:, :, 0:2], 0.0).then_inc(cleared, 1)
                            dve.wait_ge(cleared, 1 + 2 * layer)
                        add_halves(ff, lambda t: gate_in[:, t, 2:], lp)

                    unit(ff, evac, lp, done=CH if first else RING)
                    dve.wait_ge(evacuated, more_e + UT * (ff + 1))
                    V.tensor_tensor(gate_in[:, :, 2:], gate_in[:, :, 2:], row_of_r(UT), ALU.mult).then_inc(ffn_scaled, 1)
                    dve.wait_ge(ffn_scaled, scaled + 1)
                    dve.wait_ge(cw_ready, f + (NF * layer + 1))
                    for t in range(UT):
                        ins = V.tensor_scalar(gate[:, t, :], gate_in[:, t, 2:], cw[:, t, 2:3], cw[:, t, 3:4],
                                              ALU.mult, ALU.add)
                    ins.then_inc(conv_step, 1)
                    g0 = first_chunk(ff + 1)
                    for w in (1, 0):
                        split(g0 + RING + 1 - w, more)
                        dve.wait_ge(conv_step, steps + (2 - w))
                        for t in range(UT):
                            ins = V.scalar_tensor_tensor(gate[:, t, :], gate_in[:, t, w:w + S], cw[:, t, w:w + 1],
                                                         gate[:, t, :], ALU.mult, ALU.add)
                        ins.then_inc(conv_step, 1)
                    for c in range(RING + 2, CH + RING - 1):
                        split(g0 + c, more)
                    up = gate_in
                    dve.wait_ge(conv_step, steps + 3)
                    add_halves(ff + 1, lambda t: up[:, t, 2:], lp)
                    split(g0 + CH + RING - 1, more)
                    dve.wait_ge(evacuated, more_e + UT * (ff + 2))
                    V.tensor_tensor(up[:, :, 2:], up[:, :, 2:], row_of_r(UT), ALU.mult).then_inc(ffn_scaled, 1)
                    dve.wait_ge(ffn_scaled, scaled + 2)
                    dve.wait_ge(gate_ready, f + (NF * layer + 1))
                    V.tensor_tensor(gate[:], gate[:], up[:, :, 2:], ALU.mult).then_inc(hid_f, 1)
                    dve.wait_ge(hid_hi, f + (NF * layer + 1))
                    V.tensor_tensor(hid[:, bass.ds(f * UT, UT), S:2 * S], gate[:],
                                    hid[:, bass.ds(f * UT, UT), 0:S].bitcast(F32), ALU.subtract).then_inc(hid_ready, 1)

                ffn_pair(ff, None, 0, True)
                with dve.Fori(0, NF - 1) as f:
                    ffn_pair(ff + 2, (f, 2 * CH, 2 * UT), f + 1)
                if layer == 0:
                    dve.wait_ge(hid_ready, NF)
                    V.memset(sq_sum[:], 0.0).then_inc(cleared, 1)
                    dve.wait_ge(cleared, 2)
                    with dve.Fori(0, 2) as i:
                        lp = (i, 2 * CHF, 2 * UT)
                        for k in range(2):
                            unit(dn + k, y_evac(dn + k, base + 4, k, 4 * layer + 3, lp), lp)
                else:
                    for k in range(4):
                        unit(dn + k, y_evac(dn + k, base + 4, k, 4 * layer + 3))
                dve.wait_ge(evacuated, UT * (dn + 4))
                norms(2 * layer + 1, 4 * layer + 3, KC1 if layer == 0 else None)


def kernel(**a):
    import concourse.bacc as bacc
    from concourse.bass_utils import run_bass_kernel_spmd

    a = {k: np.asarray(v) for k, v in a.items()}

    def chunks(w):
        k, n = w.shape
        return w.reshape(k // (CK * P), CK, P, n // UNIT, UNIT).transpose(3, 0, 2, 1, 4).reshape(n // UNIT, -1, P, CW)

    def by_partition(v):
        return np.ascontiguousarray(np.moveaxis(v.reshape(*v.shape[:-1], -1, P), -1, 0))

    hd, kd = NH * HD, GROUPS * HD
    win0, win1 = a["swa_w_in"][0], a["nsa_w_in"][0]
    parts = []
    for layer in range(2):
        if layer == 0:
            parts += [chunks(win0[:, hd:]), chunks(win0[:, :hd]), chunks(a["swa_w_o"][0])]
        else:
            parts += [chunks(win1[:, hd:hd + 6 * kd])] + [chunks(a["nsa_cmp_w1"][0, i]) for i in range(2)]
            parts += [chunks(win1[:, :hd]), chunks(a["nsa_w_o"][0])]
        gate_up = np.stack([chunks(a["ffn_w_gate"][layer]), chunks(a["ffn_w_up"][layer])], axis=1)
        parts += [gate_up, chunks(a["ffn_w_down"][layer])]
    stream = np.concatenate([p.reshape(-1, P, CW) for p in parts])
    conv = np.concatenate([a["ffn_conv_w"], a["ffn_conv_b"][:, None]], axis=1)
    conv = conv.reshape(2, 4, NF, UT, P).transpose(4, 0, 2, 3, 1).reshape(P, 2, NF, UT * 4)
    arrays = {
        "x": by_partition(a["x"][0]).transpose(0, 2, 1),
        "gains": by_partition(a["norm_g"].reshape(8, D)),
        "stream": stream,
        "b_in": by_partition(a["swa_b_in"][0]),
        "b_o": by_partition(a["swa_b_o"][0]),
        "sinks": a["swa_sinks"][0],
        "conv": conv,
        "pe": a["nsa_cmp_pe"][0].transpose(2, 0, 1),
        "b1": by_partition(a["nsa_cmp_b1"][0]),
        "w2": a["nsa_cmp_w2"][0].reshape(2, UT, P, HD).transpose(2, 0, 1, 3),
        "b2k": a["nsa_cmp_b2"][0, 0][:, None],
        "b2v": a["nsa_cmp_b2"][0, 1][None, :],
        "w_gates": win1[:, hd + 6 * kd:].reshape(KT, P, 96).transpose(1, 0, 2),
    }
    nc = bacc.Bacc("TRN2", target_bir_lowering=False, num_devices=1)
    args = {}
    for name, v in arrays.items():
        arrays[name] = v = np.ascontiguousarray(v)
        args[name] = nc.dram_tensor(f"in_{name}", v.shape, mybir.dt.from_np(v.dtype), kind="ExternalInput").ap()
    out = nc.dram_tensor("out_y", [P, KT, S], F32, kind="ExternalOutput").ap()
    build_program(nc, out=out, **args)
    r = run_bass_kernel_spmd(nc, [{f"in_{k}": v for k, v in arrays.items()}], core_ids=[0])
    got = r.results[0]["out_y"]
    return got.transpose(2, 1, 0).reshape(1, S, D)
```

```python
from contextlib import ExitStack

import numpy as np

import concourse.bass as bass
from concourse import mybir

F32 = mybir.dt.float32
F32R = mybir.dt.float32r
ALU = mybir.AluOpType
ACT = mybir.ActivationFunctionType

P = 128
S = 256
D = 2048
F = 5632
HD = 64
NH = 32
GROUPS = 4
HPG = NH // GROUPS
KT = D // P
FT = F // P
UNIT = 512
UT = UNIT // P
NF = F // UNIT
CK = 2
CW = CK * UNIT
RING = 4
CH = KT // CK
CHF = FT // CK
WINDOW = 128
CMP_LEN, CMP_STRIDE = 32, 16
NC = (S - CMP_LEN) // CMP_STRIDE + 1
EPS = 1e-6
FAR = 1e30
NO_KEY = 1e20
CAUSAL = S // 2 * 3
TT = S // P
NP = 16

KV0, Q0, O0, FF0, DN0 = 0, 1, 5, 9, 31
KC1, KS1, KW1, WK1, WV1, Q1, O1, FF1, DN1 = 35, 36, 37, 38, 39, 40, 44, 48, 70
UNITS = 74

LAG = 3


def first_chunk(u):
    longer = min(max(u - DN0, 0), 4) + min(max(u - DN1, 0), 4)
    return CH * u + (CHF - CH) * longer


CHUNKS = first_chunk(UNITS)


def attention_items(layer):
    if layer == 0:
        return [(i, "swa") for i in range(HPG)]
    return [(0, "cmp")] + [(i, k) for i in range(HPG) for k in ("sel", "win")]


def attention_slots(layer, last):
    steps = len(attention_items(layer)) + LAG + 2
    lo, hi = (0, 23) if last else (1, 30)
    at = [[] for _ in range(CH * UT)]
    for s in range(steps):
        at[lo + s * (hi - lo) // (steps - 1)].append(s)
    return at


def build_program(nc, x, gains, stream, b_in, b_o, sinks, conv, pe, b1, w2, b2k, b2v, w_gates, out):
    with ExitStack() as ctx:
        def sb(name, shape, dt=F32, c=ctx):
            return c.enter_context(nc.sbuf_tensor(name, [P] + shape if isinstance(shape, list) else shape, dt))

        def sem(name):
            return ctx.enter_context(nc.semaphore(name))

        sets = [ctx.enter_context(nc.psum_tensor(f"set{i}", [P, UT, 512], F32)) for i in range(2)]
        ps_scores = [sets[1][:, 0, :], sets[1][:, 1, :]]
        ps_turned = sets[1][:, 2, :]
        ps_o = sets[1][:, 3, :]
        ps_mean = sets[0][:, 0, 0:S]
        ps_mean_x = [sets[1][:, 1, 0:S] if n % 2 else sets[0][:, 1, 0:S] for n in range(4)]

        raw = sb("raw", [RING, CW])
        whi = sb("whi", [RING, CW], F32R)
        wlo = sb("wlo", [RING, CW], F32R)
        xT = sb("xT", [KT, S])
        half = sb("half", [2, UT, S])
        ones = sb("ones", [P])
        ident = sb("ident", [P])
        root = sb("root", [S])
        rnorm = sb("rnorm", [S])
        g_sb = sb("g_sb", [8, KT])
        conv_sb = sb("conv_sb", [2, NF, 4 * UT])
        b_in_sb = sb("b_in_sb", [20])
        b_q = sb("b_q", [16])
        b_o_sb = sb("b_o_sb", [KT])
        sinks_sb = sb("sinks_sb", [NH])
        neg_sinks = sb("neg_sinks", [NH])
        b1_sb = sb("b1_sb", [2, UT])
        b2k_sb = sb("b2k_sb", [1])
        b2v_sb = sb("b2v_sb", [HD])
        pe_sb = sb("pe_sb", [2, CMP_LEN])
        eps = sb("eps", [1])
        spare = sb("spare", [1])

        with ExitStack() as c:
            hs = sb("hs", [KT, 2 * S], F32R, c)
        with ExitStack() as c:
            sb("under_y", [KT, S], F32, c)
            y = sb("y", [KT, S], F32, c)
        sb("hold_h", [KT * 2 * S], F32R)

        with ExitStack() as c:
            hid = sb("hid", [FT, 2 * S], F32R, c)
            gate_in = sb("gate_in", [UT, S + 2], F32, c)
            gate = sb("gate", [UT, S], F32, c)
            cw = sb("cw", [UT, 4], F32, c)
        with ExitStack() as c:
            sb("under_squares", [FT, 2 * S], F32, c)
            squares = sb("squares", [UT, S], F32, c)
            sq_sum = sb("sq_sum", [UT, S], F32, c)
        with ExitStack() as c:
            with ExitStack() as c2:
                os_ = sb("os", [KT, 2 * S], F32R, c2)
            with ExitStack() as c2:
                wg_split = sb("wg_split", [KT, 2, 96], F32R, c2)
                blocks = [sb(f"blocks{i}", [KT, 2, GROUPS * NC], F32R, c2) for i in range(2)]
                kc_raw = sb("kc_raw", [2, 2, S], F32, c2)
            sb("hold_o", [KT * 2 * S], F32R, c)
            with ExitStack() as c2:
                qg = sb("qg", [UT, S], F32, c2)
            with ExitStack() as c2:
                block_f = sb("block_f", [KT, GROUPS * NC], F32, c2)
            sb("hold_q", [UT * S], F32, c)
            k_raw = sb("k_raw", [2, 2, S], F32, c)
            v_raw = sb("v_raw", [2, 2, S], F32, c)
            k_dup = sb("k_dup", [2, GROUPS, S], F32, c)
            v_nat = sb("v_nat", [2, TT, S], F32, c)
            k_g = sb("k_g", [2, S], F32, c)
            v_g = sb("v_g", [2, TT, HD], F32, c)
            kc_all = sb("kc_all", [GROUPS * 2 * NP], F32, c)
            vc_all = sb("vc_all", [GROUPS * HD], F32, c)
            kc_g = sb("kc_g", [2 * NP], F32, c)
            repeat = sb("repeat", [HPG * NP], F32, c)
            vc_rep = sb("vc_rep", [GROUPS * HD], F32, c)
            own_head = sb("own_head", [HPG], F32, c)
            gates = sb("gates", [TT, 96], F32, c)
            gates_g = sb("gates_g", [TT, 24], F32, c)
            sinks_g = sb("sinks_g", [HPG], F32, c)
            neg_sinks_g = sb("neg_sinks_g", [HPG], F32, c)
            dist = sb("dist", [CAUSAL], F32, c)
            bias = sb("bias", [HPG, CAUSAL], F32, c)
            bias_c = sb("bias_c", [TT, HPG, NP], F32, c)
            with ExitStack() as c2:
                scored = sb("scored", [2, CAUSAL], F32, c2)
                probs = sb("probs", [LAG, CAUSAL], F32, c2)
                turned = sb("turned", [2, CAUSAL], F32, c2)
            with ExitStack() as c2:
                wg_raw = sb("wg_raw", [KT, 96], F32, c2)
            sb("hold_s", [(4 + LAG) * CAUSAL], F32, c)
            neg_max = sb("neg_max", [2, TT], F32, c)
            sums = sb("sums", [2, TT], F32, c)
            sink_e = sb("sink_e", [2, TT], F32, c)
            total = sb("total", [2, TT], F32, c)
            recip = sb("recip", [2, TT], F32, c)
            neg_r = sb("neg_r", [TT], F32, c)
            cmp_z = sb("cmp_z", [UT, GROUPS * NC], F32, c)
            low_c = sb("low_c", [TT, HPG], F32, c)
            sum_c = sb("sum_c", [TT, HPG], F32, c)
            with ExitStack() as c2:
                cmp_h = sb("cmp_h", [2, UT, GROUPS * NC], F32, c2)
                w2k_sb = sb("w2k_sb", [UT, P], F32, c2)
                w2v_sb = sb("w2v_sb", [UT, HD], F32, c2)
            with ExitStack() as c2:
                vc_g = sb("vc_g", [UT, 2, HD], F32, c2)
                probs_c = sb("probs_c", [TT, HPG, NP], F32, c2)
                turned_c = sb("turned_c", [S], F32, c2)

        raw_in = [sem(f"raw_in{i}") for i in range(RING)]
        hi_ready, lo_ready, chunk_used = sem("hi_ready"), sem("lo_ready"), sem("chunk_used")
        half_ready, evacuated = sem("half_ready"), sem("evacuated")
        const_in, late_in, filled = sem("const_in"), sem("late_in"), sem("filled")
        x_in = [sem(f"x_in{q}") for q in range(4)]
        prepared = sem("prepared")
        x_ready, sq_ready, sq_used, mean_ready = sem("x_ready"), sem("sq_ready"), sem("sq_used"), sem("mean_ready")
        root_ready, rnorm_ready = sem("root_ready"), sem("rnorm_ready")
        hf_ready, h_hi_ready, h_ready = sem("hf_ready"), sem("h_hi_ready"), sem("h_ready")
        y_sq_ready, sq_sum_ready, y_scaled = sem("y_sq_ready"), sem("sq_sum_ready"), sem("y_scaled")
        k_dup_ready, v_turned, v_ready = sem("k_dup_ready"), sem("v_turned"), sem("v_ready")
        staged, bias_ready = sem("staged"), sem("bias_ready")
        scores_ready, scores_read, exp_ready = sem("scores_ready"), sem("scores_read"), sem("exp_ready")
        total_ready, recip_ready, probs_ready = sem("total_ready"), sem("recip_ready"), sem("probs_ready")
        probs_turned, turned_copied = sem("probs_turned"), sem("turned_copied")
        o_ready, o_hi_ready, o_read = sem("o_ready"), sem("o_hi_ready"), sem("o_read")
        cw_ready, conv_step, gate_ready = sem("cw_ready"), sem("conv_step"), sem("gate_ready")
        hid_f, hid_hi, hid_ready = sem("hid_f"), sem("hid_hi"), sem("hid_ready")
        block_built, block_hi, block_ready = sem("block_built"), sem("block_hi"), sem("block_ready")
        cmp_h_ready, cleared = sem("cmp_h_ready"), sem("cleared")
        wg_hi, wg_ready, kc_done, gate_dot, kc_ready = sem("wg_hi"), sem("wg_ready"), sem("kc_done"), sem("gate_dot"), sem("kc_ready")
        vc_ready, gate_exp, gate_plus, gates_ready = sem("vc_ready"), sem("gate_exp"), sem("gate_plus"), sem("gates_ready")
        rnorm_turned, neg_r_ready, q_summed = sem("rnorm_turned"), sem("neg_r_ready"), sem("q_summed")
        vc_rep_done = sem("vc_rep_done")
        cmp_made, vc_rep_ready, v_staged, cmp_step = sem("cmp_made"), sem("vc_rep_ready"), sem("v_staged"), sem("cmp_step")
        summed, ffn_scaled = sem("summed"), sem("ffn_scaled")
        passed_dve, passed_pool = sem("passed_dve"), sem("passed_pool")
        out_ready, out_done = sem("out_ready"), sem("out_done")

        N_CONST = 11

        def items_before(layer, g=0):
            return (0 if layer == 0 else GROUPS * HPG) + g * len(attention_items(layer))

        def bias_before(layer):
            return 0 if layer == 0 else HPG + 3 * HPG

        n_bias = [HPG, HPG + 1]
        n_staged = [3, 4]

        def staged_after(layer, g):
            return (0 if layer == 0 else GROUPS * n_staged[0]) + n_staged[layer] * (g + 1)

        def set_of(u):
            if u in (KV0, KC1, KW1, WV1):
                return 1
            if Q0 <= u <= O0 or Q1 <= u <= O1 or u in (KS1, WK1):
                return 0
            base = next(b for b in (DN1, FF1, O1, DN0, FF0, O0) if u >= b)
            return (u - base) % 2

        def before_in_set(u):
            for v in range(u - 1, -1, -1):
                if set_of(v) == set_of(u):
                    return v
            return None

        block = ctx.enter_context(nc.Block())

        @block.sync
        def _(sp):
            for q in range(4):
                sp.dma_start(xT[:, q * 4:(q + 1) * 4, :], x[:, q * 4:(q + 1) * 4, :]).then_inc(x_in[q], 16)
            consts = [(g_sb[:], gains), (conv_sb[:], conv), (b_in_sb[:], b_in), (b_o_sb[:], b_o),
                      (sinks_sb[:], sinks.partition_broadcast(P)), (b1_sb[:], b1), (b2v_sb[0:1, :], b2v)]
            for h in range(2):
                half_p = slice(h * HD, (h + 1) * HD)
                consts += [(pe_sb[half_p], pe), (b2k_sb[half_p, :], b2k)]
            assert len(consts) == N_CONST
            for s in range(RING):
                sp.dma_start(raw[:, s, :], stream[s]).then_inc(raw_in[s], 16)
                for dst, src in (consts[0:1], [], [], consts[1:])[s]:
                    sp.dma_start(dst, src).then_inc(const_in, 16)
            turns = stream.rearrange("(n s) p c -> n s p c", s=RING)
            with sp.Fori(0, CHUNKS // RING - 1) as n:
                for s in range(RING):
                    sp.wait_ge(lo_ready, n * RING + (s + 1))
                    sp.dma_start(raw[:, s, :], turns[n + 1, s]).then_inc(raw_in[s], 16)
            for c in range(CH):
                sp.wait_ge(out_ready, c + 1)
                sp.dma_start(out[:, c * CK:(c + 1) * CK, :], xT[:, c * CK:(c + 1) * CK, :]).then_inc(out_done, 16)
            sp.wait_ge(out_done, 16 * CH)

        @block.gpsimd
        def _(pool):
            nc.gpsimd.memset(ones[:], 1.0).then_inc(filled, 1)
            nc.gpsimd.memset(eps[:], EPS).then_inc(filled, 1)
            nc.gpsimd.memset(ident[:], 0.0).then_inc(filled, 1)
            pool.wait_ge(filled, 3)
            nc.gpsimd.affine_select(out=ident[:], in_=ident[:], compare_op=ALU.not_equal, fill=1.0, base=0,
                                    pattern=[[-1, P]], channel_multiplier=1).then_inc(filled, 1)
            pool_sem = [0]
            made = sem("made")

            def step(ins):
                pool_sem[0] += 1
                ins.then_inc(made, 1)
                pool.wait_ge(made, pool_sem[0])

            def causal(t, window):
                step(nc.gpsimd.affine_select(out=t[:, 0:P], in_=t[:, 0:P], compare_op=ALU.is_ge, fill=FAR,
                                             base=0, pattern=[[-1, P]], channel_multiplier=1))
                last = nc.gpsimd.affine_select(out=t[:, P:], in_=t[:, P:], compare_op=ALU.is_ge, fill=FAR,
                                               base=P, pattern=[[-1, S]], channel_multiplier=1)
                if window:
                    step(last)
                    last = nc.gpsimd.affine_select(out=t[:, P:], in_=t[:, P:], compare_op=ALU.is_ge, fill=FAR,
                                                   base=WINDOW - 1 - P, pattern=[[1, S]], channel_multiplier=-1)
                return last

            def bias_tables(layer):
                step(nc.gpsimd.iota(dist[:, 0:P], pattern=[[-1, P]], base=0, channel_multiplier=1,
                                    allow_small_or_imprecise_dtypes=True))
                step(nc.gpsimd.iota(dist[:, P:], pattern=[[-1, S]], base=P, channel_multiplier=1,
                                    allow_small_or_imprecise_dtypes=True))
                for i in range(HPG):
                    slope = float(np.exp2(np.float32(-8.0 * (i + 1) / NH)))
                    step(nc.gpsimd.tensor_scalar(bias[:, i, :], dist[:], slope, 1.0, ALU.mult, ALU.mult))
                    causal(bias[:, i, :], layer == 0).then_inc(bias_ready, 1)
                if layer == 1:
                    step(nc.gpsimd.iota(dist[:, 0:2 * NP].rearrange("p (t n) -> p t n", t=TT),
                                        pattern=[[P, TT], [-CMP_STRIDE, NP]], base=1 - CMP_LEN, channel_multiplier=1,
                                        allow_small_or_imprecise_dtypes=True))
                    for i in range(HPG):
                        slope = float(np.exp2(np.float32(-8.0 * (i + 1) / NH)))
                        step(nc.gpsimd.tensor_scalar(bias_c[:, :, i, :], dist[:, 0:2 * NP].rearrange("p (t n) -> p t n", t=TT),
                                                     slope, 1.0, ALU.mult, ALU.mult))
                    nc.gpsimd.affine_select(out=bias_c[:], in_=bias_c[:], compare_op=ALU.is_ge, fill=FAR, base=1 - CMP_LEN,
                                            pattern=[[P, TT], [0, HPG], [-CMP_STRIDE, NP]],
                                            channel_multiplier=1).then_inc(bias_ready, 1)
                    step(nc.gpsimd.memset(kc_all[:], 0.0))
                    step(nc.gpsimd.tensor_copy(repeat[0:NC].rearrange("p (h n) -> p h n", h=HPG),
                                               ident[0:NC, 0:NP].unsqueeze(1).to_broadcast([NC, HPG, NP])))
                    step(nc.gpsimd.memset(own_head[:], 1.0))
                    step(nc.gpsimd.affine_select(out=own_head[:], in_=own_head[:], compare_op=ALU.is_ge, fill=0.0, base=0,
                                                 pattern=[[-NP, HPG]], channel_multiplier=1))
                    nc.gpsimd.affine_select(out=own_head[:], in_=own_head[:], compare_op=ALU.is_ge, fill=0.0,
                                            base=NP - 1, pattern=[[NP, HPG]], channel_multiplier=-1).then_inc(cmp_made, 1)
                    pool.wait_ge(cmp_made, 1)

            def stage(layer, g):
                cp = nc.gpsimd.tensor_copy
                before = items_before(layer, g)
                pool.wait_ge(scores_ready, before)
                cp(k_g[:, 0, :], k_dup[:, 0, g, :]).then_inc(staged, 1)
                if layer == 1:
                    cp(k_g[:, 1, :], k_dup[:, 1, g, :]).then_inc(staged, 1)
                    cp(kc_g[:], kc_all[:, bass.ds(g * 2 * NP, 2 * NP)]).then_inc(staged, 1)
                    pool.wait_ge(probs_ready, before)
                    cp(gates_g[:], gates[:, :, bass.ds(g * 24, 24)]).then_inc(staged, 1)
                else:
                    pool.wait_ge(exp_ready, before)
                    cp(sinks_g[:], sinks_sb[:, bass.ds(g * HPG, HPG)]).then_inc(staged, 1)
                    cp(neg_sinks_g[:], neg_sinks[:, bass.ds(g * HPG, HPG)]).then_inc(staged, 1)
                pool.wait_ge(o_ready, before)
                cp(v_g[:, 0, :, :], v_nat[:, 0, :, bass.ds(g * HD, HD)]).then_inc(v_staged, 1)
                if layer == 1:
                    nc.gpsimd.tensor_tensor(vc_g[:].rearrange("p a b d -> p (a b) d"),
                                            vc_rep[:, bass.ds(g * HD, HD)].unsqueeze(1).to_broadcast([P, HPG, HD]),
                                            own_head[:].unsqueeze(2).to_broadcast([P, HPG, HD]),
                                            ALU.mult).then_inc(v_staged, 1)
                    cp(v_g[:, 1, :, :], v_nat[:, 1, :, bass.ds(g * HD, HD)]).then_inc(v_staged, 1)

            for layer in range(2):
                if layer == 1:
                    pool.wait_ge(chunk_used, first_chunk(KC1))
                bias_tables(layer)
                pool.wait_ge(k_dup_ready, 1 if layer == 0 else 3)
                pool.wait_ge(v_ready, 1 if layer == 0 else 3)
                if layer == 0:
                    pool.wait_ge(prepared, 1)
                else:
                    pool.wait_ge(kc_ready, 1)
                    pool.wait_ge(gates_ready, 1)
                    pool.wait_ge(vc_rep_ready, 1)
                stage(layer, 0)
                items = attention_items(layer)
                with pool.Fori(0, GROUPS - 1) as g:
                    for n, (i, kind) in enumerate(items):
                        if kind == "sel":
                            continue
                        pool.wait_ge(scores_read, g * len(items) + (items_before(layer) + n + 1))
                        pool.sem_inc(passed_pool, 1)
                        t = bias_c[:].rearrange("p a b n -> p (a b n)") if kind == "cmp" else bias[:, i, :]
                        nc.gpsimd.tensor_scalar(t, t, 0.25, 1.0, ALU.mult, ALU.mult).then_inc(bias_ready, 1)
                    stage(layer, g + 1)
                ff = FF0 if layer == 0 else FF1
                pool.wait_ge(chunk_used, first_chunk(ff))
                nc.gpsimd.tensor_copy(cw[:].rearrange("p a b -> p (a b)"), conv_sb[:, layer, 0, :]).then_inc(cw_ready, 1)
                with pool.Fori(1, NF) as f:
                    pool.wait_ge(conv_step, f * 3 + layer * 3 * NF)
                    nc.gpsimd.tensor_copy(cw[:].rearrange("p a b -> p (a b)"),
                                          conv_sb[:, layer, f, :]).then_inc(cw_ready, 1)

        @block.tensor
        def _(pe):
            mm = nc.tensor.matmul

            def chunk(c, last_c, g, slot, u, rhs, width, kt0, at, tile_before=None):
                w = width
                for t in range(UT):
                    if tile_before:
                        tile_before(c * UT + t)
                    if c == 0 and at is not None:
                        pe.wait_ge(evacuated, at + t)
                    if t == 0:
                        pe.wait_ge(lo_ready, g + 1)
                    bank = sets[set_of(u)][:, t, :]
                    for j in range(CK):
                        cols = slice(j * UNIT + t * P, j * UNIT + (t + 1) * P)
                        first, final = c == 0 and j == 0, c == last_c and j == CK - 1
                        r = rhs(kt0 + j)

                        def high():
                            return mm(bank[:, 0:2 * w], whi[:, slot, cols], r, start=first, stop=final)

                        def low():
                            return mm(bank[:, w:2 * w], wlo[:, slot, cols], r[:, 0:w], start=False, stop=False)

                        if final:
                            low()
                            last = high()
                        else:
                            high()
                            last = low()
                last.then_inc(chunk_used, 1)

            def unit(u, source, lp=None, width=S, waits=None, tile_before=None, after_chunk=None):
                n = CHF if source is hid else CH
                v = before_in_set(u)
                more_g, more_e = (lp[0] * lp[1], lp[0] * lp[2]) if lp else (0, 0)
                at = None if v is None else more_e + (UT * v + 1)
                for c in range(n):
                    g0 = first_chunk(u) + c
                    if waits:
                        waits(c)
                    chunk(c, n - 1, more_g + g0, g0 % RING, u, lambda kt: source[:, kt, :], width, CK * c, at,
                          tile_before)
                    if after_chunk:
                        after_chunk(c)

            def sum_squares(out, tile, first, last):
                for t in range(UT):
                    ins = mm(out, ones[:], tile[:, t, :], start=first and t == 0, stop=last and t == UT - 1)
                return ins

            def x_squares(n, q):
                pe.wait_ge(sq_ready, 4 * n + q + 1)
                ins = sum_squares(ps_mean_x[n], sq_sum if q % 2 else squares, q == 0, q == 3)
                ins.then_inc(sq_used if q < 3 else mean_ready, 1)

            def x_squares_after(n):
                return lambda c: x_squares(n, (1, 3, 5, 6).index(c)) if c in (1, 3, 5, 6) else None

            def postnorm(n):
                pe.wait_ge(sq_sum_ready, 3 * n + 3)
                sum_squares(ps_mean, sq_sum, True, False)
                for t in range(UT):
                    pe.wait_ge(y_sq_ready, 7 * n + 3 + (t + 1))
                    ins = mm(ps_mean, ones[:], squares[:, t, :], start=False, stop=t == UT - 1)
                ins.then_inc(mean_ready, 1)

            def h_waits(n):
                return lambda c: pe.wait_ge(h_ready, c // 2 + 1 if n == 0 else 4 + CH * (n - 1) + (c + 1))

            def attention(layer, u_q, g, last):
                items = attention_items(layer)
                ib = items_before(layer) + g * len(items)
                pairs = 16 * layer + 4 * g
                at = attention_slots(layer, last)

                def scores(s):
                    i, kind = items[s]
                    hp = slice((i % 2) * HD, (i % 2) * HD + HD)
                    if s == 0:
                        pe.wait_ge(staged, staged_after(layer, g))
                    if kind == "swa" and i % 2 == 0:
                        pe.wait_ge(evacuated, u_q + (i // 2 + 1 - UT))
                    if s >= 2:
                        pe.wait_ge(scores_read, ib + (s - 1))
                    q = qg[hp, i // 2, :]
                    b = ps_scores[s % 2]
                    if kind == "cmp":
                        for p in range(HPG // 2):
                            pe.wait_ge(evacuated, u_q + (p + 1 - UT))
                            for t in range(TT):
                                ins = mm(b[:, t * P + p * 2 * NP:t * P + (p + 1) * 2 * NP], qg[:, p, t * P:(t + 1) * P],
                                         kc_g[:], start=True, stop=True)
                    else:
                        k = k_g[hp, 1 if kind == "win" else 0, :]
                        mm(b[:, 0:P], q[:, 0:P], k[:, 0:P], start=True, stop=True)
                        ins = mm(b[:, P:CAUSAL], q[:, P:S], k, start=True, stop=True)
                    ins.then_inc(scores_ready, 1)

                def turn(s):
                    kind = items[s][1]
                    pe.wait_ge(probs_ready, ib + (s + 1))
                    if s >= 1:
                        pe.wait_ge(turned_copied, ib + s)
                    e = probs[:, s % LAG, :]
                    if kind == "cmp":
                        for t in range(TT):
                            ins = nc.tensor.transpose(ps_turned[:, t * P:(t + 1) * P],
                                                      probs_c[:, t].rearrange("p a n -> p (a n)"), ident[:])
                    else:
                        for t in range(3):
                            ins = nc.tensor.transpose(ps_turned[:, t * P:(t + 1) * P], e[:, t * P:(t + 1) * P], ident[:])
                    ins.then_inc(probs_turned, 1)

                def outputs(s):
                    i, kind = items[s]
                    hp = slice((i % 2) * HD, (i % 2) * HD + HD)
                    pe.wait_ge(turned_copied, ib + (s + 1))
                    starts = kind == "cmp" or kind == "sel" and i % 2 == 0 and i > 0
                    if s == 0:
                        pe.wait_ge(v_staged, g + 1 if layer == 0 else g * 3 + GROUPS + 3)
                    if starts or kind == "swa" and i % 2 == 0:
                        pe.wait_ge(o_read, 1 + pairs + i // 2)
                    if starts:
                        rows = slice(i // 2 * 2 * NP, (i // 2 + 1) * 2 * NP)
                        ins = mm(ps_o[:, 0:S], vc_g[rows, i // 2].rearrange("p b d -> p (b d)"), turned_c[rows, :],
                                 start=True, stop=False)
                    e = turned[:, s % 2, :]
                    if kind != "cmp":
                        v = v_g[:, 1 if kind == "win" else 0]
                        mm(ps_o[hp, 0:S], v[:, 0, :], e[:, 0:S], start=kind == "swa", stop=False)
                        ins = mm(ps_o[hp, P:S], v[:, 1, :], e[:, S:CAUSAL], start=False, stop=kind != "sel")
                    ins.then_inc(o_ready, 1)

                def before(tile):
                    for s in at[tile]:
                        if LAG <= s < len(items) + LAG:
                            turn(s - LAG)
                        if s < len(items):
                            scores(s)
                        if LAG + 1 <= s < len(items) + LAG + 1:
                            outputs(s - LAG - 1)

                return before

            def turn_values(which, b):
                for tt in range(TT):
                    for f in range(2):
                        ins = nc.tensor.transpose(sets[1][:, b, tt * S + f * P:tt * S + (f + 1) * P],
                                                  v_raw[:, which, f, tt * P:(tt + 1) * P], ident[:])
                ins.then_inc(v_turned, 1)

            def after_q0(layer):
                def after(c):
                    if layer == 1 and c == CH - 1:
                        pe.wait_ge(vc_ready, 1)
                        pe.wait_ge(cmp_made, 1)
                        pe.wait_ge(v_ready, 3)
                        mm(sets[1][:, 0, 0:GROUPS * HD], repeat[0:NC, :], vc_all[0:NC, :],
                           start=True, stop=True).then_inc(vc_rep_done, 1)
                    if c != 5:
                        return
                    if layer == 0:
                        pe.wait_ge(evacuated, UT * (KV0 + 1))
                        turn_values(0, 0)
                        return
                    pe.wait_ge(evacuated, UT * (WV1 + 1))
                    turn_values(0, 0)
                    turn_values(1, 1)
                    pe.wait_ge(cmp_h_ready, 2)
                    pe.wait_ge(late_in, 16 * 4)
                    for t in range(UT):
                        ins = mm(ps_turned[:, 0:GROUPS * NC], w2k_sb[:, t, :], cmp_h[:, 0, t, :],
                                 start=t == 0, stop=t == UT - 1)
                    ins.then_inc(kc_done, 1)
                    for g in range(GROUPS):
                        o = ps_o[0:NC, g * HD:(g + 1) * HD]
                        for t in range(UT):
                            mm(o, cmp_h[:, 1, t, g * NC:(g + 1) * NC], w2v_sb[:, t, :], start=t == 0, stop=False)
                        ins = mm(o, ones[0:1, 0:NC], b2v_sb[0:1, :], start=False, stop=True)
                    pe.wait_ge(wg_ready, 1)
                    for tt in range(TT):
                        ins = nc.tensor.transpose(ps_turned[:, S + tt * P:S + (tt + 1) * P],
                                                  rnorm[:, tt * P:(tt + 1) * P], ident[:])
                    ins.then_inc(rnorm_turned, 1)
                    for tt in range(TT):
                        o = ps_o[:, S + tt * 96:S + (tt + 1) * 96]
                        for kt in range(KT):
                            hi = hs[:, kt, tt * P:(tt + 1) * P]
                            lo = hs[:, kt, S + tt * P:S + (tt + 1) * P]
                            mm(o, lo, wg_split[:, kt, 0, :], start=kt == 0, stop=False)
                            mm(o, hi, wg_split[:, kt, 1, :], start=False, stop=False)
                            ins = mm(o, hi, wg_split[:, kt, 0, :], start=False, stop=kt == KT - 1)
                    ins.then_inc(gate_dot, 1)
                return after

            for layer in range(2):
                q0, o0, ff, dn = ((Q0, O0, FF0, DN0), (Q1, O1, FF1, DN1))[layer]
                hw = h_waits(2 * layer)
                if layer == 0:
                    pe.wait_ge(filled, 4)
                    for q in range(4):
                        x_squares(0, q)
                    unit(KV0, hs, waits=hw)
                else:
                    unit(KC1, hs, waits=hw, after_chunk=x_squares_after(2))
                    pe.wait_ge(root_ready, 5)
                    unit(KS1, hs)
                    unit(KW1, hs)
                    for n, u in enumerate((WK1, WV1)):
                        pe.wait_ge(block_ready, n + 1)
                        unit(u, blocks[n][:].rearrange("p k a b -> p k (a b)"), width=GROUPS * NC)
                unit(q0, hs, after_chunk=after_q0(layer))
                if layer == 1:
                    pe.wait_ge(kc_ready, 1)
                    pe.wait_ge(vc_rep_ready, 1)
                    pe.wait_ge(gate_exp, 1)
                pe.wait_ge(v_ready, 1 if layer == 0 else 3)
                with pe.Fori(0, GROUPS - 1) as g:
                    unit(q0 + 1, hs, lp=(g, CH, UT), tile_before=attention(layer, g * UT + UT * (q0 + 1), g, False))

                def o_waits(c):
                    if c >= 6:
                        pe.wait_ge(o_read, 1 + 16 * layer + CK * c + 2)
                    elif c == 0:
                        pe.wait_ge(o_read, 1 + 16 * layer + 12)

                g = GROUPS - 1
                unit(o0, os_, waits=o_waits, tile_before=attention(layer, UT * (q0 + g + 1), g, True))
                for u in range(o0 + 1, o0 + 4):
                    unit(u, os_)
                postnorm(2 * layer)
                unit(ff, hs, waits=h_waits(2 * layer + 1), after_chunk=x_squares_after(2 * layer + 1))
                pe.wait_ge(root_ready, 4 * layer + 3)
                unit(ff + 1, hs)
                with pe.Fori(0, NF - 1) as f:
                    for u in (ff + 2, ff + 3):
                        unit(u, hs, lp=(f, 2 * CH, 2 * UT))

                def hid_waits(c):
                    if c % 2 == 0 and c // 2 >= NF - 2:
                        pe.wait_ge(hid_ready, NF * layer + c // 2 + 1)
                    elif c == 0:
                        pe.wait_ge(hid_ready, NF * layer + NF - 2)

                for u in range(dn, dn + 4):
                    unit(u, hid, waits=hid_waits if u == dn else None)
                postnorm(2 * layer + 1)

        @block.scalar
        def _(act):
            A = nc.scalar.activation
            def split(g0, more=0, turn=0):
                slot = g0 % RING
                act.wait_ge(raw_in[slot], turn + 16 * (g0 // RING + 1))
                if g0 >= RING:
                    act.wait_ge(chunk_used, more + (g0 - RING + 1))
                A(whi[:, slot, :], raw[:, slot, :], ACT.Copy).then_inc(hi_ready, 1)

            def loop_terms(lp):
                return (lp[0] * lp[1], lp[0] * (lp[1] // RING * 16), lp[0] * lp[2]) if lp else (0, 0, 0)

            def unit_first_half(u, lp=None, bias_of=None, scale=1.0, width=S, by_tile=False):
                more, _, more_e = loop_terms(lp)
                n = CHF if (DN0 <= u < DN0 + 4 or u >= DN1) else CH
                act.wait_ge(chunk_used, more + (first_chunk(u) + n))
                st = set_of(u)
                if bias_of is None:
                    if scale == 1.0 and not by_tile:
                        A(half[:, st, :, 0:width], sets[st][:, :, 0:width], ACT.Copy).then_inc(half_ready, UT)
                    else:
                        for t in range(UT):
                            A(half[:, st, t, :], sets[st][:, t, 0:S], ACT.Copy, scale=scale).then_inc(half_ready, 1)
                else:
                    for t in range(UT):
                        A(half[:, st, t, :], sets[st][:, t, 0:S], ACT.Identity, bias=bias_of(t),
                          scale=scale).then_inc(half_ready, 1)

            def unit(u, evac, lp=None, done=RING):
                more, turn, _ = loop_terms(lp)
                n = CHF if (DN0 <= u < DN0 + 4 or u >= DN1) else CH
                g0 = first_chunk(u)
                last = u == UNITS - 1
                for c in range(done, n + (0 if last else RING - 1)):
                    split(g0 + c, more, turn)
                evac()
                if not last:
                    split(g0 + n + RING - 1, more, turn)

            def finish_norm(mean, k):
                A(spare[:], eps[:], ACT.Sqrt)
                act.wait_ge(mean_ready, k + 1)
                A(root[:], mean, ACT.Sqrt, bias=eps[:], scale=1.0 / D).then_inc(root_ready, 1)

            def x_squares(n, q):
                if q >= 2:
                    act.wait_ge(sq_used, 3 * n + q - 1)
                A(sq_sum[:] if q % 2 else squares[:], xT[:, q * 4:(q + 1) * 4, :], ACT.Square).then_inc(sq_ready, 1)

            def first_norm():
                for q in range(4):
                    act.wait_ge(x_in[q], 16)
                    x_squares(0, q)
                split(0)
                act.wait_ge(filled, 4)
                finish_norm(ps_mean_x[0], 0)
                for g in range(1, RING):
                    split(g)
                for q in range(4):
                    act.wait_ge(hf_ready, q + 1)
                    A(hs[:, q * 4:(q + 1) * 4, 0:S], half[:, q % 2], ACT.Copy).then_inc(h_hi_ready, 1)

            def prenorm(n, gain, u):
                g0 = first_chunk(u)
                for c in range(CH):
                    act.wait_ge(x_ready, CH * (n - 1) + c + 1)
                    for kt in range(c * CK, (c + 1) * CK):
                        ins = A(hs[:, kt, 0:S], xT[:, kt, :], ACT.Copy, scale=g_sb[:, gain, kt:kt + 1])
                    ins.then_inc(h_hi_ready, 1)
                    if c % 2:
                        x_squares(n, c // 2)
                        for ahead in ((), (4,), (5,), (6, 7))[c // 2]:
                            split(g0 + ahead)

            def y_evac(u, n, k, bias_of=None):
                def evac():
                    unit_first_half(u, None, bias_of, by_tile=k == 3)
                    if k >= 1:
                        act.wait_ge(sq_sum_ready, 3 * n + k)
                    if k < 3:
                        act.wait_ge(evacuated, UT * (u + 1))
                        A(squares[:], y[:, k * UT:(k + 1) * UT, :], ACT.Square).then_inc(y_sq_ready, 1)
                        return
                    for t in range(UT):
                        act.wait_ge(evacuated, UT * u + (t + 1))
                        A(squares[:, t, :], y[:, k * UT + t, :], ACT.Square).then_inc(y_sq_ready, 1)
                return evac

            def attention(layer, g, last):
                items = attention_items(layer)
                ib = items_before(layer) + g * len(items)
                pairs = 16 * layer + 4 * g
                at = attention_slots(layer, last)

                def copy_turned(s):
                    act.wait_ge(probs_turned, ib + (s + 1))
                    if s >= 2:
                        act.wait_ge(o_ready, ib + (s - 1))
                    if items[s][1] == "cmp":
                        act.wait_ge(o_ready, ib)
                        A(turned_c[:], ps_turned[:, 0:S], ACT.Copy).then_inc(turned_copied, 1)
                    else:
                        A(turned[:, s % 2, :], ps_turned[:, 0:CAUSAL], ACT.Copy).then_inc(turned_copied, 1)

                def exponents(s):
                    i, kind = items[s]
                    if kind == "cmp":
                        act.wait_ge(cmp_step, g * 6 + 3)
                        A(probs_c[:], probs_c[:], ACT.Exp, scale=-1.0).then_inc(exp_ready, 1)
                        return
                    act.wait_ge(scores_read, ib + (s + 1))
                    b = s % 2
                    ends = (0, P, CAUSAL)
                    for t in range(TT):
                        cols = slice(ends[t], ends[t + 1])
                        ins = A(probs[:, s % LAG, cols], scored[:, b, cols], ACT.Exp, bias=neg_max[:, b, t:t + 1],
                                scale=-1.0, accum_out=sums[:, b, t:t + 1])
                    if kind == "swa":
                        ins = A(sink_e[:, b, :], neg_max[:, b, :], ACT.Exp, bias=sinks_g[:, i:i + 1])
                    ins.then_inc(exp_ready, 1)

                def pair_high(s):
                    p = items[s][0] // 2
                    act.wait_ge(o_ready, ib + (s + 1))
                    A(os_[:, bass.ds(g * 4 + p, 1), 0:S].rearrange("p a b -> p (a b)"), ps_o[:, 0:S],
                      ACT.Copy).then_inc(o_hi_ready, 1)

                def step(tile):
                    for s in at[tile]:
                        if s == 0:
                            act.wait_ge(staged, staged_after(layer, g))
                        o = s - LAG - 2
                        if o >= 0 and items[o][0] % 2 == 1 and items[o][1] in ("swa", "win"):
                            pair_high(o)
                        if LAG <= s < len(items) + LAG:
                            copy_turned(s - LAG)
                        if s < len(items):
                            exponents(s)

                return step

            def attention_unit(u, evac, step, lp=None):
                more, turn, _ = loop_terms(lp)
                g0 = first_chunk(u)
                for tile in range(CH * UT):
                    step(tile)
                    if tile >= UT and tile % UT == 0:
                        split(g0 + RING + tile // UT - 1, more, turn)
                evac()
                split(g0 + CH + RING - 1, more, turn)

            for layer in range(2):
                q0, o0, ff, dn = ((Q0, O0, FF0, DN0), (Q1, O1, FF1, DN1))[layer]
                if layer == 0:
                    first_norm()
                    act.wait_ge(const_in, 16 * N_CONST)
                    unit(KV0, lambda: unit_first_half(KV0, bias_of=lambda t: b_in_sb[:, 16 + t:17 + t]))
                else:
                    prenorm(2, 4, KC1)

                    def kc_evac():
                        finish_norm(ps_mean_x[2], 4)
                        act.dma_start(wg_raw[:], w_gates).then_inc(late_in, 16)
                        act.dma_start(w2k_sb[:, :, 0:HD], w2[:, 0]).then_inc(late_in, 16)
                        act.dma_start(w2k_sb[:, :, HD:P], w2[:, 0]).then_inc(late_in, 16)
                        act.dma_start(w2v_sb[:], w2[:, 1]).then_inc(late_in, 16)
                        unit_first_half(KC1)

                    unit(KC1, kc_evac, done=CH)
                    for n, u in enumerate((KS1, KW1)):
                        unit(u, lambda u=u: unit_first_half(u))
                        act.wait_ge(block_built, n + 1)
                        A(blocks[n][:, :, 0, :], block_f[:], ACT.Copy).then_inc(block_hi, 1)
                        if n == 0:
                            act.wait_ge(late_in, 64)
                            A(wg_split[:, :, 0, :], wg_raw[:], ACT.Copy).then_inc(wg_hi, 1)
                    for n, u in enumerate((WK1, WV1)):
                        def evac(u=u, n=n):
                            unit_first_half(u, width=GROUPS * NC)
                            act.wait_ge(evacuated, UT * (u + 1))
                            A(cmp_h[:, n], cmp_z[:], ACT.Gelu_apprx_tanh).then_inc(cmp_h_ready, 1)
                        unit(u, evac)

                def after_values():
                    if layer == 0:
                        act.wait_ge(v_turned, 1)
                        A(v_nat[:, 0].rearrange("p a b -> p (a b)"), sets[1][:, 0, :], ACT.Copy).then_inc(v_ready, 1)
                        return
                    for w in range(2):
                        act.wait_ge(v_turned, 2 + w)
                        A(v_nat[:, w].rearrange("p a b -> p (a b)"), sets[1][:, w, :], ACT.Copy).then_inc(v_ready, 1)
                    act.wait_ge(kc_done, 1)
                    act.wait_ge(cmp_made, 1)
                    for par in range(2):
                        hp = slice(par * HD, (par + 1) * HD)
                        ins = A(kc_all[hp].rearrange("p (g a n) -> p g a n", g=GROUPS, a=2)[:, :, par, 0:NC],
                                ps_turned[hp, 0:GROUPS * NC].rearrange("p (g n) -> p g n", g=GROUPS),
                                ACT.Identity, bias=b2k_sb[hp])
                    ins.then_inc(kc_ready, 1)
                    act.wait_ge(gate_dot, 1)
                    A(vc_all[0:NC, :], ps_o[0:NC, 0:S], ACT.Copy).then_inc(vc_ready, 1)
                    act.wait_ge(neg_r_ready, 1)
                    for tt in range(TT):
                        ins = A(gates[:, tt, :], ps_o[:, S + tt * 96:S + (tt + 1) * 96], ACT.Exp,
                                scale=neg_r[:, tt:tt + 1])
                    ins.then_inc(gate_exp, 1)

                def q_evac(u, lp=None):
                    if layer == 1:
                        return lambda: unit_first_half(u, lp, by_tile=True)
                    if lp is None:
                        return lambda: unit_first_half(u, lp, scale=-HD ** -0.5, bias_of=lambda t: b_q[:, t:t + 1])
                    return lambda: unit_first_half(
                        u, lp, scale=-HD ** -0.5, bias_of=lambda t: b_q[:, bass.ds(lp[0] * UT + (UT + t), 1)])

                if layer == 0:
                    act.wait_ge(prepared, 1)

                def q0_evac():
                    after_values()
                    q_evac(q0)()
                    if layer == 1:
                        act.wait_ge(vc_rep_done, 1)
                        A(vc_rep[:], sets[1][:, 0, 0:GROUPS * HD], ACT.Copy).then_inc(vc_rep_ready, 1)

                unit(q0, q0_evac)
                with act.Fori(0, GROUPS - 1) as g:
                    lp = (g, CH, UT)
                    attention_unit(q0 + 1, q_evac(q0 + 1, lp), attention(layer, g, False), lp)
                bias_of = (lambda k: lambda t: b_o_sb[:, k * UT + t:k * UT + t + 1]) if layer == 0 else lambda k: None
                n = 2 * layer
                attention_unit(o0, y_evac(o0, n, 0, bias_of(0)), attention(layer, GROUPS - 1, True))
                for k in range(1, 4):
                    unit(o0 + k, y_evac(o0 + k, n, k, bias_of(k)))
                finish_norm(ps_mean, 4 * layer + 1)
                prenorm(2 * layer + 1, 4 * layer + 2, ff)

                def ffn_pair(ff, lp, f, first=False):
                    more, turn, _ = loop_terms(lp)

                    def evac():
                        if first:
                            finish_norm(ps_mean_x[2 * layer + 1], 4 * layer + 2)
                        unit_first_half(ff, lp)

                    unit(ff, evac, lp, done=CH if first else RING)
                    g0 = first_chunk(ff + 1)
                    for c in range(RING, CH):
                        split(g0 + c, more, turn)
                    act.wait_ge(conv_step, f * 3 + (3 * NF * layer + 3))
                    A(gate[:], gate[:], ACT.Silu).then_inc(gate_ready, 1)
                    for c in range(CH, CH + RING - 1):
                        split(g0 + c, more, turn)
                    unit_first_half(ff + 1, lp)
                    split(g0 + CH + RING - 1, more, turn)
                    act.wait_ge(hid_f, f + (NF * layer + 1))
                    A(hid[:, bass.ds(f * UT, UT), 0:S], gate[:], ACT.Copy).then_inc(hid_hi, 1)

                ffn_pair(ff, None, 0, True)
                with act.Fori(0, NF - 1) as f:
                    ffn_pair(ff + 2, (f, 2 * CH, 2 * UT), f + 1)
                for k in range(4):
                    unit(dn + k, y_evac(dn + k, n + 1, k))
                finish_norm(ps_mean, 4 * layer + 3)

        @block.vector
        def _(dve):
            V = nc.vector
            def split(g0, more=0):
                slot = g0 % RING
                dve.wait_ge(hi_ready, more + (g0 + 1))
                V.tensor_tensor(wlo[:, slot, :], raw[:, slot, :], whi[:, slot, :].bitcast(F32),
                                ALU.subtract).then_inc(lo_ready, 1)

            def loop_terms(lp):
                return (lp[0] * lp[1], lp[0] * lp[2]) if lp else (0, 0)

            def unit(u, evac, lp=None, done=RING):
                more, _ = loop_terms(lp)
                n = CHF if (DN0 <= u < DN0 + 4 or u >= DN1) else CH
                g0 = first_chunk(u)
                last = u == UNITS - 1
                for c in range(done, n + (0 if last else RING - 1)):
                    split(g0 + c, more)
                evac()
                if not last:
                    split(g0 + n + RING - 1, more)

            def add_halves(u, dst, lp=None, scale=None, width=S):
                _, more_e = loop_terms(lp)
                st = set_of(u)
                for t in range(UT):
                    dve.wait_ge(half_ready, more_e + (UT * u + t + 1))
                    b, h = sets[st][:, t, width:2 * width], half[:, st, t, 0:width]
                    if scale is None:
                        ins = V.tensor_tensor(dst(t), h, b, ALU.add)
                    else:
                        ins = V.scalar_tensor_tensor(dst(t), b, scale, h, ALU.mult, ALU.add)
                    ins.then_inc(evacuated, 1)

            def finish_norm(k):
                dve.wait_ge(root_ready, k + 1)
                V.reciprocal(rnorm[:], root[:]).then_inc(rnorm_ready, 1)
                dve.wait_ge(rnorm_ready, k + 1)

            def first_norm():
                n, gain = 0, 0
                split(0)
                dve.wait_ge(const_in, 16 * N_CONST)
                V.tensor_scalar(b_q[:], b_in_sb[:, 0:16], -HD ** -0.5, None, ALU.mult).then_inc(o_read, 1)
                V.tensor_scalar(neg_sinks[:], sinks_sb[:], -1.0, None, ALU.mult).then_inc(prepared, 1)
                finish_norm(0)

                def scaled(q):
                    for t in range(UT):
                        ins = V.scalar_tensor_tensor(half[:, q % 2, t, :], xT[:, q * 4 + t, :],
                                                     g_sb[:, gain, q * 4 + t:q * 4 + t + 1], rnorm[:], ALU.mult, ALU.mult)
                    ins.then_inc(hf_ready, 1)

                def low(q):
                    dve.wait_ge(h_hi_ready, 4 * n + q + 1)
                    V.tensor_tensor(hs[:, q * 4:(q + 1) * 4, S:2 * S], half[:, q % 2],
                                    hs[:, q * 4:(q + 1) * 4, 0:S].bitcast(F32), ALU.subtract).then_inc(h_ready, 1)

                scaled(0)
                split(1)
                scaled(1)
                for q in range(4):
                    low(q)
                    if q < 2:
                        split(q + 2)
                    if q + 2 < 4:
                        dve.wait_ge(h_ready, 4 * n + q + 1)
                        scaled(q + 2)

            def row_of_r(tiles):
                return rnorm[:].unsqueeze(1).to_broadcast([P, tiles, S])

            def low_of_h(n, gain, c):
                dve.wait_ge(h_hi_ready, 4 + CH * (n - 1) + (c + 1))
                for kt in range(c * CK, (c + 1) * CK):
                    ins = V.scalar_tensor_tensor(hs[:, kt, S:2 * S], xT[:, kt, :], g_sb[:, gain, kt:kt + 1],
                                                 hs[:, kt, 0:S].bitcast(F32), ALU.mult, ALU.subtract)
                ins.then_inc(h_ready, 1)

            def norms(n, gain, u=None):
                dve.wait_ge(y_scaled, 12 * n + 4)
                finish_norm(2 * n + 1)
                for c in range(CH):
                    part = slice(c * CK, (c + 1) * CK)
                    V.tensor_tensor(y[:, part, :], y[:, part, :], row_of_r(CK), ALU.mult).then_inc(y_scaled, 1)
                    if u is not None and c >= 1:
                        low_of_h(n + 1, gain + 1, c - 1)
                    dve.wait_ge(y_scaled, 12 * n + 4 + c + 1)
                    V.tensor_tensor(xT[:, part, :], xT[:, part, :], y[:, part, :],
                                    ALU.add).then_inc(x_ready if u is not None else out_ready, 1)
                    if u is not None:
                        for ahead in {5: (4,), 7: (5,)}.get(c, ()):
                            split(first_chunk(u) + ahead)
                if u is not None:
                    low_of_h(n + 1, gain + 1, CH - 1)
                    split(first_chunk(u) + 6)
                    split(first_chunk(u) + 7)

            def times_r(u, t, k):
                dve.wait_ge(evacuated, UT * (u + 1))
                V.tensor_tensor(t, t, row_of_r(t.shape[1]), ALU.mult).then_inc(summed, 1)
                dve.wait_ge(summed, k)

            def y_evac(u, n, k):
                def evac():
                    add_halves(u, lambda t: y[:, k * UT + t, :])
                    if k < 3:
                        dve.wait_ge(y_sq_ready, 7 * n + k + 1)
                        if k == 0:
                            V.tensor_copy(sq_sum[:], squares[:]).then_inc(sq_sum_ready, 1)
                        else:
                            dve.wait_ge(sq_sum_ready, 3 * n + k)
                            V.tensor_tensor(sq_sum[:], sq_sum[:], squares[:], ALU.add).then_inc(sq_sum_ready, 1)
                    for t in range(UT):
                        if k == 3:
                            dve.wait_ge(y_sq_ready, 7 * n + 3 + (t + 1))
                        kt = k * UT + t
                        ins = V.tensor_scalar(y[:, kt, :], y[:, kt, :], g_sb[:, 2 * n + 1, kt:kt + 1], None, ALU.mult)
                    ins.then_inc(y_scaled, 1)
                return evac

            def attention(layer, g, last):
                items = attention_items(layer)
                ib = items_before(layer) + g * len(items)
                at = attention_slots(layer, last)
                tb = 8 * GROUPS * layer + g * HPG

                def add_bias(s):
                    i, kind = items[s]
                    b = s % 2
                    dve.wait_ge(scores_ready, ib + (s + 1))
                    if s == 0:
                        dve.wait_ge(bias_ready, bias_before(layer) + n_bias[layer] * (g + 1))
                        dve.wait_ge(staged, staged_after(layer, g))
                    if kind == "cmp":
                        dve.wait_ge(probs_turned, ib)
                        flat = probs_c[:].rearrange("p a b n -> p (a b n)")
                        V.tensor_tensor(flat, ps_scores[b][:, 0:TT * HPG * NP], bias_c[:].rearrange("p a b n -> p (a b n)"),
                                        ALU.add).then_inc(scores_read, 1)
                        dve.wait_ge(scores_read, ib + (s + 1))
                        V.tensor_reduce(low_c[:], probs_c[:], mybir.AxisListType.X, ALU.min).then_inc(cmp_step, 1)
                        dve.wait_ge(cmp_step, g * 6 + 1)
                        V.tensor_scalar(low_c[:], low_c[:], NO_KEY, None, ALU.min).then_inc(cmp_step, 1)
                        dve.wait_ge(cmp_step, g * 6 + 2)
                        V.tensor_tensor(probs_c[:], probs_c[:], low_c[:].unsqueeze(3).to_broadcast([P, TT, HPG, NP]),
                                        ALU.subtract).then_inc(cmp_step, 1)
                        return
                    dve.sem_inc(passed_dve, 1)
                    ends = (0, P, CAUSAL)
                    table = bias
                    for t in range(TT):
                        cols = slice(ends[t], ends[t + 1])
                        ins = V.tensor_tensor_reduce(
                            out=scored[:, b, cols], in0=ps_scores[b][:, cols], in1=table[:, i, cols], scale=1.0,
                            scalar=neg_sinks_g[:, i:i + 1] if kind == "swa" else NO_KEY,
                            op0=ALU.add, op1=ALU.min, accum_out=neg_max[:, b, t:t + 1])
                    ins.then_inc(scores_read, 1)

                def normalize(s):
                    i, kind = items[s]
                    b = s % 2
                    dve.wait_ge(exp_ready, ib + (s + 1))
                    if kind == "cmp":
                        V.tensor_reduce(sum_c[:], probs_c[:], mybir.AxisListType.X, ALU.add).then_inc(cmp_step, 1)
                        dve.wait_ge(cmp_step, g * 6 + 4)
                        V.tensor_scalar(sum_c[:], sum_c[:], 1e-30, None, ALU.max).then_inc(cmp_step, 1)
                        dve.wait_ge(cmp_step, g * 6 + 5)
                        V.reciprocal(sum_c[:], sum_c[:]).then_inc(recip_ready, 1)
                        dve.wait_ge(recip_ready, ib + (s + 1))
                        gates_c = gates_g[:].rearrange("p t (h k) -> p t h k", k=3)[:, :, :, 0]
                        V.tensor_tensor(sum_c[:], sum_c[:], gates_c, ALU.mult).then_inc(cmp_step, 1)
                        dve.wait_ge(cmp_step, g * 6 + 6)
                        V.tensor_tensor(probs_c[:], probs_c[:], sum_c[:].unsqueeze(3).to_broadcast([P, TT, HPG, NP]),
                                        ALU.mult).then_inc(probs_ready, 1)
                        return
                    tot = sums
                    if kind == "swa":
                        V.tensor_tensor(total[:, b, :], sums[:, b, :], sink_e[:, b, :], ALU.add).then_inc(total_ready, 1)
                        tot = total
                        dve.wait_ge(total_ready, tb + (i + 1))
                    V.reciprocal(recip[:, b, :], tot[:, b, :]).then_inc(recip_ready, 1)
                    dve.wait_ge(recip_ready, ib + (s + 1))
                    ends = (0, P, CAUSAL)
                    which = {"sel": 1, "win": 2}
                    for t in range(TT):
                        e = probs[:, s % LAG, ends[t]:ends[t + 1]]
                        r = recip[:, b, t:t + 1]
                        if kind == "swa":
                            ins = V.tensor_scalar(e, e, r, None, ALU.mult)
                        else:
                            c = 3 * i + which[kind]
                            ins = V.tensor_scalar(e, e, r, gates_g[:, t, c:c + 1], ALU.mult, ALU.mult)
                    ins.then_inc(probs_ready, 1)

                def pair_low(s):
                    p = items[s][0] // 2
                    dve.wait_ge(o_hi_ready, 16 * layer + 4 * g + (p + 1))
                    at_pair = os_[:, bass.ds(g * 4 + p, 1), :].rearrange("p a b -> p (a b)")
                    V.tensor_tensor(at_pair[:, S:2 * S], ps_o[:, 0:S], at_pair[:, 0:S].bitcast(F32),
                                    ALU.subtract).then_inc(o_read, 1)

                def step(tile):
                    for s in at[tile]:
                        o = s - LAG - 2
                        if o >= 0 and items[o][0] % 2 == 1 and items[o][1] in ("swa", "win"):
                            pair_low(o)
                        if s < len(items):
                            add_bias(s)
                        if 1 <= s < len(items) + 1:
                            normalize(s - 1)

                return step

            def attention_unit(u, evac, step, lp=None):
                more, _ = loop_terms(lp)
                g0 = first_chunk(u)
                for tile in range(CH * UT):
                    step(tile)
                    if tile >= UT and tile % UT == 2:
                        split(g0 + RING + tile // UT - 1, more)
                evac()
                split(g0 + CH + RING - 1, more)

            def duplicate(which):
                for j in range(GROUPS):
                    src = k_raw[(j % 2) * HD:(j % 2) * HD + HD, which, j // 2, :]
                    for h in range(2):
                        ins = V.tensor_copy(k_dup[h * HD:(h + 1) * HD, which, j, :], src)
                ins.then_inc(k_dup_ready, 1)

            def build_blocks(n):
                for j in range(GROUPS):
                    hp = (j % 2) * HD
                    for par in range(2):
                        a = kc_raw[hp:hp + HD, n, j // 2, par:par + 1]
                        kv = bass.AP(tensor=a.tensor, offset=a.offset, ap=[a.ap[0], [2, KT], [CMP_STRIDE, NC]])
                        emb = pe_sb[hp:hp + HD, n, par:CMP_LEN:2].unsqueeze(2).to_broadcast([HD, KT, NC])
                        ins = V.tensor_tensor(block_f[par * HD:(par + 1) * HD, :, j * NC:(j + 1) * NC], kv, emb, ALU.add)
                ins.then_inc(block_built, 1)

            for layer in range(2):
                q0, o0, ff, dn = ((Q0, O0, FF0, DN0), (Q1, O1, FF1, DN1))[layer]
                if layer == 0:
                    for q in range(4):
                        dve.wait_ge(x_in[q], 16)
                    first_norm()
                    unit(KV0, lambda: add_halves(KV0, lambda t: (k_raw if t < 2 else v_raw)[:, 0, t % 2, :]))
                    dve.wait_ge(evacuated, UT * (KV0 + 1))
                    duplicate(0)
                else:
                    def kc_evac():
                        finish_norm(4)
                        add_halves(KC1, lambda t: kc_raw[:, t // 2, t % 2, :])

                    unit(KC1, kc_evac, done=CH)
                    times_r(KC1, kc_raw[:].rearrange("p a b s -> p (a b) s"), 1)
                    build_blocks(0)
                    for n, u in enumerate((KS1, KW1)):
                        unit(u, lambda: add_halves(u, lambda t: (k_raw if t < 2 else v_raw)[:, n, t % 2, :]))
                        times_r(u, k_raw[:, n], 2 * n + 2)
                        times_r(u, v_raw[:, n], 2 * n + 3)
                        duplicate(n)
                        dve.wait_ge(block_hi, n + 1)
                        V.tensor_tensor(blocks[n][:, :, 1, :], block_f[:], blocks[n][:, :, 0, :].bitcast(F32),
                                        ALU.subtract).then_inc(block_ready, 1)
                        if n == 0:
                            dve.wait_ge(block_ready, 1)
                            build_blocks(1)
                            dve.wait_ge(wg_hi, 1)
                            V.tensor_tensor(wg_split[:, :, 1, :], wg_raw[:], wg_split[:, :, 0, :].bitcast(F32),
                                            ALU.subtract).then_inc(wg_ready, 1)
                    for n, u in enumerate((WK1, WV1)):
                        w = GROUPS * NC

                        def evac():
                            for t in range(UT):
                                dve.wait_ge(half_ready, UT * (u + 1))
                                if n and t == 0:
                                    dve.wait_ge(cmp_h_ready, 1)
                                st = set_of(u)
                                V.scalar_tensor_tensor(cmp_z[:, t, :], sets[st][:, t, w:2 * w], b1_sb[:, n, t:t + 1],
                                                       half[:, st, t, 0:w], ALU.add, ALU.add).then_inc(evacuated, 1)
                        unit(u, evac)

                def q_dst(t):
                    return qg[:, t, :]

                def q_evac(u, lp):
                    if layer == 0:
                        add_halves(u, q_dst, lp, scale=-HD ** -0.5)
                        return
                    more_e = lp[0] * lp[2] if lp else 0
                    st = set_of(u)

                    def add(t):
                        dve.wait_ge(half_ready, more_e + (UT * u + t + 1))
                        V.tensor_tensor(half[:, st, t, :], half[:, st, t, :], sets[st][:, t, S:2 * S],
                                        ALU.add).then_inc(q_summed, 1)

                    add(0)
                    for t in range(UT):
                        if t + 1 < UT:
                            add(t + 1)
                        dve.wait_ge(q_summed, more_e + (UT * (u - q0) + t + 1))
                        V.scalar_tensor_tensor(qg[:, t, :], half[:, st, t, :], -HD ** -0.5, rnorm[:],
                                               ALU.mult, ALU.mult).then_inc(evacuated, 1)

                def q0_evac():
                    if layer == 1:
                        dve.wait_ge(rnorm_turned, 1)
                        dve.wait_ge(kc_ready, 1)
                        V.tensor_scalar(neg_r[:], ps_turned[:, S:2 * S].rearrange("p (t c) -> p t c", t=TT)[:, :, 0],
                                        -1.0, None, ALU.mult).then_inc(neg_r_ready, 1)
                        dve.wait_ge(gate_exp, 1)
                        V.tensor_scalar(gates[:], gates[:], 1.0, None, ALU.add).then_inc(gate_plus, 1)
                        dve.wait_ge(gate_plus, 1)
                        V.reciprocal(gates[:], gates[:]).then_inc(gates_ready, 1)
                    q_evac(q0, None)

                unit(q0, q0_evac)
                with dve.Fori(0, GROUPS - 1) as g:
                    lp = (g, CH, UT)
                    attention_unit(q0 + 1, lambda: q_evac(q0 + 1, lp),
                                   attention(layer, g, False), lp)
                attention_unit(o0, y_evac(o0, 2 * layer, 0), attention(layer, GROUPS - 1, True))
                for k in range(1, 4):
                    unit(o0 + k, y_evac(o0 + k, 2 * layer, k))
                dve.wait_ge(evacuated, UT * (o0 + 4))
                norms(2 * layer, 4 * layer + 1, ff)

                def ffn_pair(ff, lp, f, first=False):
                    more, more_e = loop_terms(lp)
                    steps = f * 3 + 3 * NF * layer
                    scaled = f * 2 + 2 * NF * layer

                    def evac():
                        if first:
                            finish_norm(4 * layer + 2)
                            V.memset(gate_in[:, :, 0:2], 0.0).then_inc(cleared, 1)
                            dve.wait_ge(cleared, 1 + layer)
                        add_halves(ff, lambda t: gate_in[:, t, 2:], lp)

                    unit(ff, evac, lp, done=CH if first else RING)
                    dve.wait_ge(evacuated, more_e + UT * (ff + 1))
                    V.tensor_tensor(gate_in[:, :, 2:], gate_in[:, :, 2:], row_of_r(UT), ALU.mult).then_inc(ffn_scaled, 1)
                    dve.wait_ge(ffn_scaled, scaled + 1)
                    dve.wait_ge(cw_ready, f + (NF * layer + 1))
                    for t in range(UT):
                        ins = V.tensor_scalar(gate[:, t, :], gate_in[:, t, 2:], cw[:, t, 2:3], cw[:, t, 3:4],
                                              ALU.mult, ALU.add)
                    ins.then_inc(conv_step, 1)
                    g0 = first_chunk(ff + 1)
                    for w in (1, 0):
                        split(g0 + RING + 1 - w, more)
                        dve.wait_ge(conv_step, steps + (2 - w))
                        for t in range(UT):
                            ins = V.scalar_tensor_tensor(gate[:, t, :], gate_in[:, t, w:w + S], cw[:, t, w:w + 1],
                                                         gate[:, t, :], ALU.mult, ALU.add)
                        ins.then_inc(conv_step, 1)
                    for c in range(RING + 2, CH + RING - 1):
                        split(g0 + c, more)
                    up = gate_in
                    dve.wait_ge(conv_step, steps + 3)
                    add_halves(ff + 1, lambda t: up[:, t, 2:], lp)
                    split(g0 + CH + RING - 1, more)
                    dve.wait_ge(evacuated, more_e + UT * (ff + 2))
                    V.tensor_tensor(up[:, :, 2:], up[:, :, 2:], row_of_r(UT), ALU.mult).then_inc(ffn_scaled, 1)
                    dve.wait_ge(ffn_scaled, scaled + 2)
                    dve.wait_ge(gate_ready, f + (NF * layer + 1))
                    V.tensor_tensor(gate[:], gate[:], up[:, :, 2:], ALU.mult).then_inc(hid_f, 1)
                    dve.wait_ge(hid_hi, f + (NF * layer + 1))
                    V.tensor_tensor(hid[:, bass.ds(f * UT, UT), S:2 * S], gate[:],
                                    hid[:, bass.ds(f * UT, UT), 0:S].bitcast(F32), ALU.subtract).then_inc(hid_ready, 1)

                ffn_pair(ff, None, 0, True)
                with dve.Fori(0, NF - 1) as f:
                    ffn_pair(ff + 2, (f, 2 * CH, 2 * UT), f + 1)
                for k in range(4):
                    unit(dn + k, y_evac(dn + k, 2 * layer + 1, k))
                dve.wait_ge(evacuated, UT * (dn + 4))
                norms(2 * layer + 1, 4 * layer + 3, KC1 if layer == 0 else None)


def kernel(**a):
    import concourse.bacc as bacc
    from concourse.bass_utils import run_bass_kernel_spmd

    a = {k: np.asarray(v) for k, v in a.items()}

    def chunks(w):
        k, n = w.shape
        return w.reshape(k // (CK * P), CK, P, n // UNIT, UNIT).transpose(3, 0, 2, 1, 4).reshape(n // UNIT, -1, P, CW)

    def by_partition(v):
        return np.ascontiguousarray(np.moveaxis(v.reshape(*v.shape[:-1], -1, P), -1, 0))

    hd, kd = NH * HD, GROUPS * HD
    win0, win1 = a["swa_w_in"][0], a["nsa_w_in"][0]
    parts = []
    for layer in range(2):
        if layer == 0:
            parts += [chunks(win0[:, hd:]), chunks(win0[:, :hd]), chunks(a["swa_w_o"][0])]
        else:
            parts += [chunks(win1[:, hd:hd + 6 * kd])] + [chunks(a["nsa_cmp_w1"][0, i]) for i in range(2)]
            parts += [chunks(win1[:, :hd]), chunks(a["nsa_w_o"][0])]
        gate_up = np.stack([chunks(a["ffn_w_gate"][layer]), chunks(a["ffn_w_up"][layer])], axis=1)
        parts += [gate_up, chunks(a["ffn_w_down"][layer])]
    stream = np.concatenate([p.reshape(-1, P, CW) for p in parts])
    conv = np.concatenate([a["ffn_conv_w"], a["ffn_conv_b"][:, None]], axis=1)
    conv = conv.reshape(2, 4, NF, UT, P).transpose(4, 0, 2, 3, 1).reshape(P, 2, NF, UT * 4)
    arrays = {
        "x": by_partition(a["x"][0]).transpose(0, 2, 1),
        "gains": by_partition(a["norm_g"].reshape(8, D)),
        "stream": stream,
        "b_in": by_partition(a["swa_b_in"][0]),
        "b_o": by_partition(a["swa_b_o"][0]),
        "sinks": a["swa_sinks"][0],
        "conv": conv,
        "pe": a["nsa_cmp_pe"][0].transpose(2, 0, 1),
        "b1": by_partition(a["nsa_cmp_b1"][0]),
        "w2": a["nsa_cmp_w2"][0].reshape(2, UT, P, HD).transpose(2, 0, 1, 3),
        "b2k": a["nsa_cmp_b2"][0, 0][:, None],
        "b2v": a["nsa_cmp_b2"][0, 1][None, :],
        "w_gates": win1[:, hd + 6 * kd:].reshape(KT, P, 96).transpose(1, 0, 2),
    }
    nc = bacc.Bacc("TRN2", target_bir_lowering=False, num_devices=1)
    args = {}
    for name, v in arrays.items():
        arrays[name] = v = np.ascontiguousarray(v)
        args[name] = nc.dram_tensor(f"in_{name}", v.shape, mybir.dt.from_np(v.dtype), kind="ExternalInput").ap()
    out = nc.dram_tensor("out_y", [P, KT, S], F32, kind="ExternalOutput").ap()
    build_program(nc, out=out, **args)
    r = run_bass_kernel_spmd(nc, [{f"in_{k}": v for k, v in arrays.items()}], core_ids=[0])
    got = r.results[0]["out_y"]
    return got.transpose(2, 1, 0).reshape(1, S, D)
```
